# Optimizing a Trainium2 kernel written in Bass

```python
import jax, jax.numpy as jnp
from jax import lax
import numpy as np
import math

D_MODEL = 1024
BATCH = 1
SEQ = 512
DEPTH = 2

PLE_DIM = 256
HEAD_DIM = 64
N_Q_HEADS = 16
N_KV_HEADS = 4
Q_PER_KV = N_Q_HEADS // N_KV_HEADS
WINDOW = 128
BLOCK = 128
ROPE_THETA = 10000.0
ATT_Q = N_Q_HEADS * HEAD_DIM
ATT_KV = N_KV_HEADS * HEAD_DIM
RW_HEADS = 16
RW_HEAD = 64
RW_DIM = RW_HEADS * RW_HEAD
DECAY_RANK = 64
ICLR_RANK = 64
GATE_RANK = 160
RW_SHIFT_COLS = 3 * RW_DIM + DECAY_RANK + ICLR_RANK + GATE_RANK
D_IN = ATT_Q + 2 * ATT_KV + RW_SHIFT_COLS + 2 * D_MODEL
FFN_DIM = 2816
CONV_W = 3
NORM_EPS = 1e-6
GN_EPS = 64e-5


def _split(z, sizes):
    out, off = [], 0
    for s in sizes:
        out.append(z[..., off:off + s])
        off += s
    return out

def rmsnorm(x, g):
    xf = x.astype(jnp.float32)
    y = xf * lax.rsqrt(jnp.mean(xf * xf, axis=-1, keepdims=True) + NORM_EPS)
    return (y * g.astype(jnp.float32)).astype(x.dtype)

def rope(t, positions):
    half = HEAD_DIM // 2
    inv_freq = jnp.power(ROPE_THETA, -jnp.arange(half, dtype=jnp.float32) / half)
    ang = positions.astype(jnp.float32)[..., None] * inv_freq
    cos = jnp.cos(ang)[:, :, None, :]
    sin = jnp.sin(ang)[:, :, None, :]
    tf = t.astype(jnp.float32)
    t1, t2 = tf[..., :half], tf[..., half:]
    return jnp.concatenate([t1 * cos - t2 * sin, t2 * cos + t1 * sin], axis=-1).astype(t.dtype)

def sliding_window_attention(q, k, v, sinks):
    B, S = q.shape[0], q.shape[1]
    nb = S // BLOCK
    qb = q.astype(jnp.float32).reshape(B, nb, BLOCK, N_KV_HEADS, Q_PER_KV, HEAD_DIM)

    def kv_blocks(t):
        t = t.astype(jnp.float32)
        prev = jnp.pad(t, ((0, 0), (BLOCK, 0), (0, 0), (0, 0)))[:, :S]
        return jnp.concatenate([prev.reshape(B, nb, BLOCK, N_KV_HEADS, HEAD_DIM),
                                t.reshape(B, nb, BLOCK, N_KV_HEADS, HEAD_DIM)], axis=2)

    kb, vb = kv_blocks(k), kv_blocks(v)
    s = jnp.einsum('bnqhgd,bnkhd->bnhgqk', qb, kb) * (HEAD_DIM ** -0.5)
    qi = jnp.arange(BLOCK)[:, None]
    kj = jnp.arange(2 * BLOCK)[None, :]
    dist = qi + BLOCK - kj
    band = (dist >= 0) & (dist < WINDOW)
    kpos = jnp.arange(nb)[:, None, None] * BLOCK - BLOCK + kj[None]
    mask = band[None] & (kpos >= 0)
    s = jnp.where(mask[None, :, None, None], s, -jnp.inf)
    sink = sinks.astype(jnp.float32).reshape(N_KV_HEADS, Q_PER_KV)[None, None, :, :, None, None]
    m = jnp.maximum(jnp.max(s, axis=-1, keepdims=True), sink)
    pr = jnp.exp(s - m)
    pr = pr / (jnp.sum(pr, axis=-1, keepdims=True) + jnp.exp(sink - m))
    o = jnp.einsum('bnhgqk,bnkhd->bnqhgd', pr, vb)
    return o.reshape(B, S, ATT_Q).astype(q.dtype)

def rwkv7_scan(r, w, k, v, a, b):
    B, S, H, N = r.shape

    def step(state, inp):
        r_t, w_t, k_t, v_t, a_t, b_t = inp
        sa = jnp.einsum('bhvk,bhk->bhv', state, a_t)
        state = (state * w_t[:, :, None, :] + sa[..., None] * b_t[:, :, None, :]
                 + v_t[..., None] * k_t[:, :, None, :])
        return state, jnp.einsum('bhvk,bhk->bhv', state, r_t)

    xs = tuple(jnp.moveaxis(t.astype(jnp.float32), 1, 0) for t in (r, w, k, v, a, b))
    s0 = jnp.zeros((B, H, N, N), jnp.float32)
    _, y = lax.scan(step, s0, xs)
    return jnp.moveaxis(y, 0, 1)

def rwkv7_time_mix(z, mu, w0, w2, a0, a2, g2, k_k, k_a, r_k, gn_w, gn_b):
    B, S = z.shape[0], z.shape[1]
    zs = z + (jnp.pad(z, ((0, 0), (1, 0), (0, 0)))[:, :S] - z) * mu
    r, k, v, wd, ad, gd = _split(zs, (RW_DIM, RW_DIM, RW_DIM, DECAY_RANK, ICLR_RANK, GATE_RANK))
    w = -jax.nn.softplus(-(w0 + jnp.tanh(wd) @ w2)) - 0.5
    decay = jnp.exp(-jnp.exp(w.astype(jnp.float32)))
    iclr = jax.nn.sigmoid(a0 + ad @ a2)
    g = jax.nn.sigmoid(gd) @ g2

    def heads(t):
        return t.astype(jnp.float32).reshape(B, S, RW_HEADS, RW_HEAD)

    kk = heads(k * k_k)
    kk = kk / jnp.maximum(jnp.sqrt(jnp.sum(kk * kk, axis=-1, keepdims=True)), 1e-12)
    k = k * (1.0 + (iclr - 1.0) * k_a)
    rh, kh, vh, ah = heads(r), heads(k), heads(v), heads(iclr)
    y = rwkv7_scan(rh, heads(decay), kh, vh, -kk, kk * ah)
    mean = jnp.mean(y, axis=-1, keepdims=True)
    var = jnp.mean(jnp.square(y - mean), axis=-1, keepdims=True)
    y = ((y - mean) * lax.rsqrt(var + GN_EPS)).reshape(B, S, RW_DIM) * gn_w + gn_b
    bonus = jnp.sum(rh * kh * r_k.astype(jnp.float32), axis=-1, keepdims=True) * vh
    out = (y + bonus.reshape(B, S, RW_DIM)) * g
    return out.astype(z.dtype)

def causal_dwconv(u, w, b):
    C = u.shape[-1]
    y = lax.conv_general_dilated(u, w[:, None, :].astype(u.dtype), window_strides=(1,),
                                 padding=[(CONV_W - 1, 0)],
                                 dimension_numbers=('NWC', 'WIO', 'NWC'),
                                 feature_group_count=C)
    return y + b

def hybrid_layer(x, p_i, positions, norm_mix_pre, w_in, att_sinks, w_o_att, rw_mu, rw_w0,
                 rw_w2, rw_a0, rw_a2, rw_g2, rw_k_k, rw_k_a, rw_r_k, rw_gn_w, rw_gn_b,
                 w_o_rw, w_out, norm_mix_post, norm_ffn_pre, w_up, conv_w, conv_b, w_down,
                 norm_ffn_post, w_ple, w_ple_gate, norm_ple):
    B, S = x.shape[0], x.shape[1]
    h = rmsnorm(x, norm_mix_pre)
    proj = h @ w_in
    q, k, v, rw, gate_a, gate_b = _split(proj, (ATT_Q, ATT_KV, ATT_KV, RW_SHIFT_COLS, D_MODEL, D_MODEL))
    q = rope(q.reshape(B, S, N_Q_HEADS, HEAD_DIM), positions)
    k = rope(k.reshape(B, S, N_KV_HEADS, HEAD_DIM), positions)
    v = v.reshape(B, S, N_KV_HEADS, HEAD_DIM)
    y_att = sliding_window_attention(q, k, v, att_sinks) @ w_o_att
    y_rw = rwkv7_time_mix(rw, rw_mu, rw_w0, rw_w2, rw_a0, rw_a2, rw_g2, rw_k_k, rw_k_a,
                          rw_r_k, rw_gn_w, rw_gn_b) @ w_o_rw
    mixed = jax.nn.sigmoid(gate_a) * y_att + jax.nn.sigmoid(gate_b) * y_rw
    x = x + rmsnorm(mixed @ w_out, norm_mix_post)
    h = rmsnorm(x, norm_ffn_pre)
    u = causal_dwconv(h @ w_up, conv_w, conv_b)
    ua, ub = _split(u, (FFN_DIM, FFN_DIM))
    x = x + rmsnorm((jax.nn.gelu(ua) * ub) @ w_down, norm_ffn_post)
    e = p_i @ w_ple
    gate = jax.nn.sigmoid(x @ w_ple_gate)
    x = x + rmsnorm(gate * e, norm_ple)
    return x

def first_inputs(seed: int = 0) -> dict:
    key = jax.random.key(seed)
    ks = iter(jax.random.split(key, 40))

    def nrm(shape, scale):
        return jax.random.normal(next(ks), shape, jnp.float32) * scale

    def gain(n):
        return 1.0 + nrm((DEPTH, n), 0.05)

    L = DEPTH
    return {
        'x': nrm((BATCH, SEQ, D_MODEL), 1.0),
        'p': nrm((DEPTH, BATCH, SEQ, PLE_DIM), 1.0),
        'positions': jnp.broadcast_to(jnp.arange(SEQ, dtype=jnp.int32)[None], (BATCH, SEQ)),
        'norm_mix_pre': gain(D_MODEL),
        'w_in': nrm((L, D_MODEL, D_IN), D_MODEL ** -0.5),
        'att_sinks': nrm((L, N_Q_HEADS), 0.5),
        'w_o_att': nrm((L, ATT_Q, D_MODEL), ATT_Q ** -0.5),
        'rw_mu': jax.random.uniform(next(ks), (L, RW_SHIFT_COLS), jnp.float32),
        'rw_w0': nrm((L, RW_DIM), 0.5),
        'rw_w2': nrm((L, DECAY_RANK, RW_DIM), DECAY_RANK ** -0.5),
        'rw_a0': nrm((L, RW_DIM), 0.5),
        'rw_a2': nrm((L, ICLR_RANK, RW_DIM), ICLR_RANK ** -0.5),
        'rw_g2': nrm((L, GATE_RANK, RW_DIM), GATE_RANK ** -0.5),
        'rw_k_k': 0.85 + nrm((L, RW_DIM), 0.1),
        'rw_k_a': 1.0 + nrm((L, RW_DIM), 0.1),
        'rw_r_k': nrm((L, RW_HEADS, RW_HEAD), 0.1),
        'rw_gn_w': gain(RW_DIM),
        'rw_gn_b': nrm((L, RW_DIM), 0.01),
        'w_o_rw': nrm((L, RW_DIM, D_MODEL), RW_DIM ** -0.5),
        'w_out': nrm((L, D_MODEL, D_MODEL), D_MODEL ** -0.5),
        'norm_mix_post': gain(D_MODEL),
        'norm_ffn_pre': gain(D_MODEL),
        'w_up': nrm((L, D_MODEL, 2 * FFN_DIM), D_MODEL ** -0.5),
        'conv_w': nrm((L, CONV_W, 2 * FFN_DIM), CONV_W ** -0.5),
        'conv_b': nrm((L, 2 * FFN_DIM), 0.01),
        'w_down': nrm((L, FFN_DIM, D_MODEL), FFN_DIM ** -0.5),
        'norm_ffn_post': gain(D_MODEL),
        'w_ple': nrm((L, PLE_DIM, D_MODEL), PLE_DIM ** -0.5),
        'w_ple_gate': nrm((L, D_MODEL, D_MODEL), D_MODEL ** -0.5),
        'norm_ple': gain(D_MODEL),
    }

def first_block(x, p, positions, norm_mix_pre, w_in, att_sinks, w_o_att, rw_mu, rw_w0, rw_w2,
              rw_a0, rw_a2, rw_g2, rw_k_k, rw_k_a, rw_r_k, rw_gn_w, rw_gn_b, w_o_rw, w_out,
              norm_mix_post, norm_ffn_pre, w_up, conv_w, conv_b, w_down, norm_ffn_post,
              w_ple, w_ple_gate, norm_ple):
    for i in range(DEPTH):
        x = hybrid_layer(x, p[i], positions, norm_mix_pre[i], w_in[i], att_sinks[i], w_o_att[i],
                         rw_mu[i], rw_w0[i], rw_w2[i], rw_a0[i], rw_a2[i], rw_g2[i], rw_k_k[i],
                         rw_k_a[i], rw_r_k[i], rw_gn_w[i], rw_gn_b[i], w_o_rw[i], w_out[i],
                         norm_mix_post[i], norm_ffn_pre[i], w_up[i], conv_w[i], conv_b[i],
                         w_down[i], norm_ffn_post[i], w_ple[i], w_ple_gate[i], norm_ple[i])
    return x


POOL_WINDOWS = (2, 4, 8, 16)
N_POOL_GROUPS = len(POOL_WINDOWS)
POOL_GROUP_DIM = D_MODEL // 8
POOL_DIM = N_POOL_GROUPS * POOL_GROUP_DIM

N_HEADS = D_MODEL // 128
QK_NOPE = 64
QK_ROPE = 32
V_DIM = 64
Q_LORA = 384
KV_LORA = 256
ATTN_DIM = N_HEADS * V_DIM
Q_BLOCK = 128

D_FF = 4 * D_MODEL

N_MOD = 6
EPS = 1e-6

IN_SPLITS = (POOL_DIM, Q_LORA, KV_LORA, QK_ROPE, D_MODEL, D_MODEL)
D_IN_2 = sum(IN_SPLITS)


def rms_norm(x, g):
    xf = x.astype(jnp.float32)
    y = xf * lax.rsqrt(jnp.mean(xf * xf, axis=-1, keepdims=True) + EPS)
    return y.astype(x.dtype) * g

def apply_rope(x, cos, sin):
    half = x.shape[-1] // 2
    x1, x2 = x[..., :half], x[..., half:]
    return jnp.concatenate([x1 * cos - x2 * sin, x2 * cos + x1 * sin], axis=-1)

def pool_mixer(u, w_pool, pool_scale):
    B, S, _ = u.shape
    t = jnp.arange(S)
    outs = []
    for g, w in enumerate(POOL_WINDOWS):
        ug = u[..., g * POOL_GROUP_DIM:(g + 1) * POOL_GROUP_DIM].astype(jnp.float32)
        cs = jnp.cumsum(ug, axis=1)
        lag = jnp.pad(cs, ((0, 0), (w, 0), (0, 0)))[:, :S]
        cnt = jnp.minimum(t + 1, w).astype(jnp.float32)[None, :, None]
        outs.append(((cs - lag) / cnt - ug).astype(u.dtype))
    p = jnp.stack(outs, axis=2)
    y = jnp.einsum('bsgc,gcd->bsgd', p, w_pool).reshape(B, S, POOL_DIM)
    return y * pool_scale

def mla(c_q_raw, c_kv_raw, k_rope_raw, q_norm_g, w_uq, kv_norm_g, w_uk, w_uv, cos, sin):
    B, S, _ = c_q_raw.shape
    c_q = rms_norm(c_q_raw, q_norm_g)
    q = jnp.einsum('bsr,rhd->bshd', c_q, w_uq)
    q_nope = q[..., :QK_NOPE]
    q_rope = apply_rope(q[..., QK_NOPE:], cos[:, :, None, :], sin[:, :, None, :])
    c_kv = rms_norm(c_kv_raw, kv_norm_g)
    k_nope = jnp.einsum('bsr,rhd->bhsd', c_kv, w_uk)
    v = jnp.einsum('bsr,rhd->bhsd', c_kv, w_uv)
    k_rope = apply_rope(k_rope_raw, cos, sin)

    nb = S // Q_BLOCK
    def to_blocks(a):
        d = a.shape[-1]
        return a.reshape(B, nb, Q_BLOCK, N_HEADS, d).transpose(1, 0, 3, 2, 4)
    qn_b = to_blocks(q_nope)
    qr_b = to_blocks(q_rope)
    starts = jnp.arange(nb, dtype=jnp.int32) * Q_BLOCK
    key_pos = jnp.arange(S, dtype=jnp.int32)
    scale = 1.0 / math.sqrt(QK_NOPE + QK_ROPE)
    neg = jnp.finfo(jnp.float32).min

    def attend(args):
        qn, qr, start = args
        s = (jnp.einsum('bhqd,bhkd->bhqk', qn, k_nope)
             + jnp.einsum('bhqd,bkd->bhqk', qr, k_rope)).astype(jnp.float32) * scale
        q_pos = start + jnp.arange(Q_BLOCK, dtype=jnp.int32)
        mask = q_pos[:, None] >= key_pos[None, :]
        p = jax.nn.softmax(jnp.where(mask, s, neg), axis=-1)
        return jnp.einsum('bhqk,bhkd->bhqd', p.astype(v.dtype), v)

    o = lax.map(attend, (qn_b, qr_b, starts))
    return o.transpose(1, 0, 3, 2, 4).reshape(B, S, ATTN_DIM)

def second_inputs(seed: int = 0) -> dict:
    key = jax.random.key(seed)
    ks = jax.random.split(key, 24)
    f32 = jnp.float32

    def dense(k, shape, fan_in, mult=1.0):
        return jax.random.normal(k, shape, f32) * (mult * fan_in ** -0.5)

    def gain(k, shape):
        return 1.0 + 0.02 * jax.random.normal(k, shape, f32)

    x = jax.random.normal(ks[0], (BATCH, SEQ, D_MODEL), f32)
    c = jax.random.normal(ks[1], (BATCH, D_MODEL), f32)
    offsets = jax.random.randint(ks[2], (BATCH, 1), 0, 1024, dtype=jnp.int32)
    positions = offsets + jnp.arange(SEQ, dtype=jnp.int32)[None, :]
    return {
        "x": x,
        "c": c,
        "positions": positions,
        "ln1_g": gain(ks[3], (DEPTH, D_MODEL)),
        "ln2_g": gain(ks[4], (DEPTH, D_MODEL)),
        "w_ada": dense(ks[5], (DEPTH, D_MODEL, N_MOD * D_MODEL), D_MODEL, 0.5),
        "b_ada": 0.01 * jax.random.normal(ks[6], (DEPTH, N_MOD * D_MODEL), f32),
        "w_in": dense(ks[7], (DEPTH, D_MODEL, D_IN_2), D_MODEL),
        "q_norm_g": gain(ks[8], (DEPTH, Q_LORA)),
        "w_uq": dense(ks[9], (DEPTH, Q_LORA, N_HEADS, QK_NOPE + QK_ROPE), Q_LORA),
        "kv_norm_g": gain(ks[10], (DEPTH, KV_LORA)),
        "w_uk": dense(ks[11], (DEPTH, KV_LORA, N_HEADS, QK_NOPE), KV_LORA),
        "w_uv": dense(ks[12], (DEPTH, KV_LORA, N_HEADS, V_DIM), KV_LORA),
        "w_pool": dense(ks[13], (DEPTH, N_POOL_GROUPS, POOL_GROUP_DIM, POOL_GROUP_DIM), POOL_GROUP_DIM),
        "pool_scale": gain(ks[14], (DEPTH, POOL_DIM)),
        "p_pool": dense(ks[15], (DEPTH, POOL_DIM, D_MODEL), POOL_DIM),
        "p_attn": dense(ks[16], (DEPTH, ATTN_DIM, D_MODEL), ATTN_DIM),
        "w_out": dense(ks[17], (DEPTH, D_MODEL, D_MODEL), D_MODEL),
        "w_ff1": dense(ks[18], (DEPTH, D_MODEL, D_FF), D_MODEL),
        "w_ff2": dense(ks[19], (DEPTH, D_FF, D_MODEL), D_FF),
        "final_g": gain(ks[20], (D_MODEL,)),
    }

def second_block(x, c, positions, ln1_g, ln2_g, w_ada, b_ada, w_in, q_norm_g, w_uq,
              kv_norm_g, w_uk, w_uv, w_pool, pool_scale, p_pool, p_attn, w_out,
              w_ff1, w_ff2, final_g):
    inv_freq = ROPE_THETA ** (-jnp.arange(0, QK_ROPE, 2, dtype=jnp.float32) / QK_ROPE)
    ang = positions.astype(jnp.float32)[..., None] * inv_freq
    cos = jnp.cos(ang).astype(x.dtype)
    sin = jnp.sin(ang).astype(x.dtype)
    c_act = jax.nn.silu(c)
    cuts = np.cumsum(IN_SPLITS)[:-1].tolist()

    for l in range(DEPTH):
        mod = c_act @ w_ada[l] + b_ada[l]
        sh1, sc1, g1, sh2, sc2, g2 = [m[:, None, :] for m in jnp.split(mod, N_MOD, axis=-1)]

        h = rms_norm(x, ln1_g[l]) * (1.0 + sc1) + sh1
        z = h @ w_in[l]
        u_pool, c_q_raw, c_kv_raw, k_rope_raw, gz_a, gz_b = jnp.split(z, cuts, axis=-1)
        y_a = pool_mixer(u_pool, w_pool[l], pool_scale[l]) @ p_pool[l]
        y_b = mla(c_q_raw, c_kv_raw, k_rope_raw, q_norm_g[l], w_uq[l], kv_norm_g[l],
                  w_uk[l], w_uv[l], cos, sin) @ p_attn[l]
        merged = jax.nn.sigmoid(gz_a) * y_a + jax.nn.sigmoid(gz_b) * y_b
        x = x + g1 * (merged @ w_out[l])

        h2 = rms_norm(x, ln2_g[l]) * (1.0 + sc2) + sh2
        x = x + g2 * (jnp.square(jax.nn.relu(h2 @ w_ff1[l])) @ w_ff2[l])

    return rms_norm(x, final_g)


def setup_inputs(seed=0):
    out = dict(first_inputs(seed))
    for name, value in second_inputs(seed + 1).items():
        if name != "x":
            out[name + "_2"] = value
    return out


def reference(
    x, p, positions, norm_mix_pre, w_in, att_sinks, w_o_att, rw_mu, rw_w0, rw_w2, rw_a0, rw_a2,
    rw_g2, rw_k_k, rw_k_a, rw_r_k, rw_gn_w, rw_gn_b, w_o_rw, w_out, norm_mix_post, norm_ffn_pre,
    w_up, conv_w, conv_b, w_down, norm_ffn_post, w_ple, w_ple_gate, norm_ple, c_2, positions_2,
    ln1_g_2, ln2_g_2, w_ada_2, b_ada_2, w_in_2, q_norm_g_2, w_uq_2, kv_norm_g_2, w_uk_2, w_uv_2,
    w_pool_2, pool_scale_2, p_pool_2, p_attn_2, w_out_2, w_ff1_2, w_ff2_2, final_g_2,
):
    x = first_block(
        x, p, positions, norm_mix_pre, w_in, att_sinks, w_o_att, rw_mu, rw_w0, rw_w2, rw_a0,
        rw_a2, rw_g2, rw_k_k, rw_k_a, rw_r_k, rw_gn_w, rw_gn_b, w_o_rw, w_out, norm_mix_post,
        norm_ffn_pre, w_up, conv_w, conv_b, w_down, norm_ffn_post, w_ple, w_ple_gate, norm_ple,
    )
    return second_block(
        x, c_2, positions_2, ln1_g_2, ln2_g_2, w_ada_2, b_ada_2, w_in_2, q_norm_g_2, w_uq_2,
        kv_norm_g_2, w_uk_2, w_uv_2, w_pool_2, pool_scale_2, p_pool_2, p_attn_2, w_out_2,
        w_ff1_2, w_ff2_2, final_g_2,
    )


_drawn_inputs = setup_inputs


def setup_inputs(seed=0):
    import zlib

    import numpy as np

    out = dict(_drawn_inputs(seed))
    spreads = {}
    factors = {'att_sinks': 4.512,
     'rw_gn_b': 5.179,
     'conv_b': 4.865,
     'ln1_g_2': 8.0,
     'ln2_g_2': 8.0,
     'b_ada_2': 6.409,
     'q_norm_g_2': 8.0,
     'w_uq_2': 5.505,
     'kv_norm_g_2': 8.0,
     'w_uk_2': 6.332,
     'pool_scale_2': 8.0,
     'final_g_2': 2.828}
    for name, (base, spread) in spreads.items():
        noise = np.random.default_rng([zlib.crc32(name.encode()), seed]).standard_normal(out[name].shape)
        drawn = base * np.exp(spread * noise) if base else spread * noise
        out[name] = __import__('jax').numpy.asarray(drawn.astype(out[name].dtype))
    for name, factor in factors.items():
        out[name] = (out[name] * factor).astype(out[name].dtype)
    return out
```

```python
from contextlib import ExitStack

import numpy as np
import concourse.bass as bass
from concourse import mybir

F32 = mybir.dt.float32
F32R = mybir.dt.float32r
I32 = mybir.dt.int32
ACT = mybir.ActivationFunctionType
ALU = mybir.AluOpType
AX = mybir.AxisListType
ADD, SUB, MUL, MAX = ALU.add, ALU.subtract, ALU.mult, ALU.max

P = 128
TOK = 512
BLK = 4
D = 1024
KD = D // P
LAYERS = 2
UNIT = 1024
RAW = 2
SLOTS = 3
PART = 8
GRING = 12
UNIT2, SLOTS2 = 2048, 3

HEADS, KV, HD = 16, 4, 64
PAIRS = 8
FFN = 2816
FT = FFN // P
NORM_EPS = 1e-6
GN_EPS = 64e-5
DECAY = float(np.exp(-0.5))
LEVELS = 7
NEG = -1e30

WINDOWS = (2, 4, 8, 16)
H2, NOPE, ROPE, VD = 8, 64, 32, 64
QK = NOPE + ROPE
QT, KVT = 3, 2
FT2 = 4 * D // P
MODS = 48

PAR1 = {}
_at = 0
for _name, _n in (("mix_pre", 8), ("mu", 27), ("w0", 8), ("a0", 8), ("kk", 8), ("ka", 8), ("rk", 8),
                  ("gnw", 8), ("gnb", 8), ("mix_post", 8), ("ffn_pre", 8), ("cw0", 44), ("cw1", 44),
                  ("cw2", 44), ("cb", 44), ("ffn_post", 8), ("ple", 8), ("sink", 64)):
    PAR1[_name] = _at
    _at += _n
NPAR1 = _at
PAR2 = {}
_at = 0
for _name, _n in (("ln1", 8), ("ln2", 8), ("bada", 48), ("qn", 3), ("kvn", 2), ("ps", 4)):
    PAR2[_name] = _at
    _at += _n
NPAR2 = _at

CONST = {}
_at = 0
for _name, _n in (("ident", 128), ("ones", 128), ("bd", 128), ("bdswap", 128), ("lvl", 7 * 128),
                  ("tmask", 256), ("amask", 256), ("cmask", 512), ("perm1", 128), ("perm2", 96),
                  ("freq1", 1), ("freq2", 1), ("invcnt", 4 * 16), ("eps6", 1), ("epsgn", 1)):
    CONST[_name] = _at
    _at += _n
NCONST = _at


class Steps:

    def __init__(self, *names):
        self.at = {n: i + 1 for i, n in enumerate(names)}
        self.n = len(names)

    def __call__(self, turn, name):
        return turn * self.n + self.at[name]


def semaphores(ctx, nc, names):
    made = [ctx.enter_context(nc.semaphore(n)) for n in names]
    return dict(zip(names, made)), sorted(m.num for m in made)


def clear_all(nc, numbers):
    first = 0
    for i, n in enumerate(numbers):
        if i + 1 == len(numbers) or numbers[i + 1] != n + 1:
            nc.multi_engine_barrier(mybir.ALL_ENGINES, sems_to_clear=range(numbers[first], n + 1))
            first = i + 1



NORM_SEMS = ("_sq", "_ss", "_rt", "_rs")


def norm_act(act, s, b, name, src, n, dim, ready=None):
    sq, ss, rt = (s[name + x] for x in NORM_SEMS[:3])
    for i in range(n):
        if ready:
            act.wait_ge(*ready(i))
        if i >= 2:
            act.wait_ge(ss, i - 1)
        act.activation(b["sq"][:, i % 2], src(i), ACT.Square).then_inc(sq, 1)
    act.wait_ge(ss, n)
    act.activation(b["rt"][:], b["ps"][:, b["norm_bank"]], ACT.Sqrt, scale=1.0 / dim,
                   bias=b["c"]("eps6")).then_inc(rt, 1)


def norm_pe(pe, s, b, name, n):
    sq, ss = (s[name + x] for x in NORM_SEMS[:2])
    for i in range(n):
        pe.wait_ge(sq, i + 1)
        pe.matmul(b["ps"][:, b["norm_bank"]], b["c"]("ones"), b["sq"][:, i % 2], start=i == 0,
                  stop=i == n - 1).then_inc(ss, 1)


def norm_dve(dve, s, name, b):
    rt, rs = (s[name + x] for x in NORM_SEMS[2:])
    dve.wait_ge(rt, 1)
    dve.reciprocal(b["rstd"][:], b["rt"][:]).then_inc(rs, 1)
    dve.wait_ge(rs, 1)


def split_matmuls(pe, ps, left, right, n, start=True, stop=True):
    last = None
    for k in range(n):
        for i, (a, c) in enumerate(((0, 0), (0, 1), (1, 0))):
            last = pe.matmul(ps, left[a](k), right[c](k), start=start and k == 0 and i == 0,
                             stop=stop and k == n - 1 and i == 2)
    return last


def tiles_of(high, low):
    return (lambda k: high[:, k]), (lambda k: low[:, k])


def columns_of(unit, n, at=0, width=P, j=0, m=P):
    def part(x):
        w = x[:, at:at + n * width].rearrange("p (k n) -> p k n", k=n)
        return lambda k: w[:, k, j:j + m]
    return part(unit[0]), part(unit[1])


class Ring:

    def __init__(self, s, b):
        self.s, self.b, self.u = s, b, 0

    def take(self, pe):
        slot = self.u % SLOTS
        self.u += 1
        pe.wait_ge(self.s["w_lo"], self.u)
        return self.b["Whi"][:, slot], self.b["Wlo"][:, slot]


class HighParts:

    def __init__(self, s, b, freed):
        self.s, self.b, self.freed, self.u = s, b, freed, 0

    def upto(self, act, n):
        while self.u < min(n, len(self.freed)):
            u = self.u
            act.wait_ge(self.s[f"w_in{u % RAW}"], 16 * (u // RAW + 1))
            if u >= SLOTS:
                act.wait_ge(*self.freed[u - SLOTS])
            act.activation(self.b["Whi"][:, u % SLOTS], self.b["raw"][:, u % RAW], ACT.Copy).then_inc(self.s["w_hi"], 1)
            self.u += 1

    def around(self, act, u):
        self.upto(act, u + SLOTS)


def low_parts(pool, s, b, first, end):
    for u in range(first, end):
        pool.wait_ge(s["w_hi"], u + 1)
        pool.tensor_tensor(b["Wlo"][:, u % SLOTS], b["raw"][:, u % RAW], b["Whi"][:, u % SLOTS].bitcast(F32), SUB) \
            .then_inc(s["w_lo"], 1)


def stream_loads(sp, s, b, dram, layer, first, end):
    for u in range(first, end):
        if u >= RAW:
            sp.wait_ge(s["w_lo"], u - RAW + 1)
        sp.dma_start(b["raw"][:, u % RAW], dram[bass.ds(layer, 1), u].rearrange("l p n -> (l p) n")) \
            .then_inc(s[f"w_in{u % RAW}"], 16)


SPLIT_SEMS = ("_t", "_hi", "_lo")


def split_act(act, s, name, b, high, n, shift=None):
    for i in range(n):
        act.wait_ge(s[name + "_t"], i + 1)
        if shift:
            act.activation(high[:, i], b["t2"][:, i % 2], ACT.Identity, bias=shift(i)).then_inc(s[name + "_hi"], 1)
        else:
            act.activation(high[:, i], b["t2"][:, i % 2], ACT.Copy).then_inc(s[name + "_hi"], 1)


def split_dve(dve, s, name, b, make, high, low, n, shift=None):
    def tile(i):
        if i >= 2:
            dve.wait_ge(s[name + "_lo"], i - 1)
        make(i, b["t2"][:, i % 2]).then_inc(s[name + "_t"], 1)

    tile(0)
    for i in range(n):
        if i + 1 < n:
            tile(i + 1)
        dve.wait_ge(s[name + "_t"], i + 1)
        dve.wait_ge(s[name + "_hi"], i + 1)
        if shift:
            dve.scalar_tensor_tensor(out=low[:, i], in0=b["t2"][:, i % 2], scalar=shift(i), in1=high[:, i].bitcast(F32),
                                     op0=ADD, op1=SUB).then_inc(s[name + "_lo"], 1)
        else:
            dve.tensor_tensor(low[:, i], b["t2"][:, i % 2], high[:, i].bitcast(F32), SUB) \
                .then_inc(s[name + "_lo"], 1)


def scaled(dve, b, src, gain):
    return lambda i, dst: dve.scalar_tensor_tensor(out=dst, in0=src[:, i], scalar=gain(i), in1=b["rstd"][:], op0=MUL, op1=MUL)


def tables(nc, b, positions, freq_col, rows, cos, sin, keep=None):
    two_pi = 2 * np.pi
    c1 = float(np.float32(6.28125))
    c2 = float(np.float32(np.float64(two_pi - c1) // 2.0 ** -21 * 2.0 ** -21))
    c3 = float(np.float32(two_pi - c1 - c2))
    magic = 12582912.0
    with ExitStack() as ctx:
        ang = ctx.enter_context(nc.sbuf_tensor("ang_" + freq_col, [P, TOK], F32))
        pos = ctx.enter_context(nc.sbuf_tensor("pos_" + freq_col, [P, TOK], I32))
        turn = ctx.enter_context(nc.sbuf_tensor("turn_" + freq_col, [P, TOK], F32))
        red = ctx.enter_context(nc.sbuf_tensor("red_" + freq_col, [P, TOK], F32))
        s, every = semaphores(ctx, nc, ["pos_in", "angle_step", "table_done"])
        with nc.Block() as block:
            @block.sync
            def _(sp):
                sp.dma_start(pos[:], positions.broadcast_to([P, TOK])).then_inc(s["pos_in"], 16)

            @block.vector
            def _(dve):
                n = [0]

                def step(ins):
                    n[0] += 1
                    ins.then_inc(s["angle_step"], 1)
                    dve.wait_ge(s["angle_step"], n[0])

                dve.wait_ge(s["pos_in"], 16)
                step(dve.tensor_copy(ang[:], pos[:]))
                step(dve.tensor_scalar(ang[:], ang[:], b["c"](freq_col), None, MUL))
                for shift, first in ((np.pi / 2, True), (0.0, False)):
                    if not first:
                        dve.wait_ge(s["table_done"], 1)
                    step(dve.tensor_scalar(turn[:], ang[:], float(1 / two_pi), float(shift / two_pi), MUL, ADD))
                    step(dve.tensor_scalar(turn[:], turn[:], magic, -magic, ADD, ADD))
                    step(dve.scalar_tensor_tensor(out=red[:], in0=turn[:], scalar=-c1, in1=ang[:], op0=MUL, op1=ADD))
                    step(dve.scalar_tensor_tensor(out=red[:], in0=turn[:], scalar=-c2, in1=red[:], op0=MUL, op1=ADD))
                    step(dve.scalar_tensor_tensor(out=red[:], in0=turn[:], scalar=-c3, in1=red[:], op0=MUL, op1=ADD))
                    if first:
                        step(dve.tensor_scalar(red[:], red[:], float(shift), None, ADD))
                    step(dve.tensor_scalar(red[:], red[:], 3.1415925, -3.1415925, ALU.min, MAX))

            @block.scalar
            def _(act):
                act.wait_ge(s["angle_step"], 9)
                act.activation(cos, red[rows], ACT.Sin).then_inc(s["table_done"], 1)
                act.wait_ge(s["angle_step"], 15)
                act.activation(sin, red[rows], ACT.Sin).then_inc(s["table_done"], 1)
        clear_all(nc, every)


GEMM = Steps("r", "k", "v", "g", "w", "a")
EV = Steps("r", "k", "v", "g", "w", "a")
MIX = Steps("dr", "r", "dk", "k", "dv", "v")
PREP_V = Steps("c0", "c1", "c2", "c3", "cm", "fe", "cx", "kkr", "big", "rn", "kk", "na", "nr", "b",
               "kf", "ks", "rk")
PREP_G = Steps("bt", "bh", "kt", "kh")
PREP_A = Steps("sqk", "en", "ep", "epx", "f", "rt")
FRONT_P = Steps("trA", "trB", "trK", "trV", *[f"T{i}" for i in range(8)])
FRONT_A = Steps("trA", "trB", "trK", "trV")
FRONT_V = Steps(*[f"T{i}" for i in range(8)])
INV_G = Steps(*[f"m{l}{h}" for l in range(LEVELS) for h in range(2)])
INV_P = Steps("X00", "X01", *[f"{m}{l}{h}" for l in range(1, 7) for m, h in
                              (("W", 0), ("W", 1), ("X", 0), ("T", 0), ("X", 1), ("T", 1))
                              if not (m == "X" and l == 6)])
INV_A = Steps("X00", "X01", *[f"W{l}{h}" for l in range(1, 7) for h in range(2)])
INV_V = Steps("T00", "T01", *[f"{m}{l}{h}" for l in range(1, 7) for h in range(2) for m in "XT"
                              if not (m == "X" and l == 6)])
TAIL_P = Steps("GV", "XA0", "XA1", "RY0", "RY1", "M", "N", "S2", "S3", "Y")
TAIL_A = Steps("GV", "XA0", "XA1", "N0", "N1")
TAIL_V = Steps("RY0", "YL0", "RY1", "YL1", "M10", "M11", "M20", "M21", "S2", "S3", "Y")
POST_P = Steps("bonus", "mean", "var")
POST_A = Steps("sq", "sd")
POST_V = Steps("bv", "d", "rr", "yn", "ya", "o", "og", "yh", "yl")

RWKV_SEMS = ["lo_hi", "lo_lo", "prep_g", "y_out", "lo_mm", "lo_z", "lo_d", "lo_mix", "lo_act", "gemm_p", "gemm_ev", "mix", "prep_v", "prep_a",
             "ssq_p", "front_p", "front_a", "front_v", "inv_g", "inv_p", "inv_a", "inv_v",
             "tail_p", "tail_a", "tail_v", "post_p", "post_a", "post_v"]


TAIL_GEMM = {"N": "r", "S2": "k"}


def ring_order():
    order = [("lo", i) for i in range(3)]
    order += [("g", 0, x) for x in GEMM.at] + [("ssq", 0), ("g", 1, "r"), ("g", 1, "k")]
    for p in range(PAIRS):
        order += [("f", p, x) for x in FRONT_P.at]
        if p + 1 < PAIRS:
            order += [("g", p + 1, x) for x in "vgwa"]
        if p:
            order += [("post", p - 1, x) for x in ("bonus", "mean")]
        if p + 1 < PAIRS:
            order += [("ssq", p + 1)]
        if p:
            order += [("post", p - 1, "var")]
        for x in TAIL_P.at:
            order.append(("t", p, x))
            if x in TAIL_GEMM and p + 2 < PAIRS:
                order.append(("g", p + 2, TAIL_GEMM[x]))
    order += [("post", PAIRS - 1, x) for x in POST_P.at]
    return {key: i for i, key in enumerate(order)}, order


RING, RING_LIST = ring_order()


def freed_count(s, key):
    if key[0] == "lo":
        return s["lo_z"], key[1] + 1
    if key[0] == "g":
        return s["gemm_ev"], EV(key[1], key[2])
    if key[0] == "ssq":
        return s["prep_a"], PREP_A(key[1], "rt")
    if key[0] == "f":
        return (s["front_a"], FRONT_A(key[1], key[2])) if key[2][0] == "t" else \
            (s["front_v"], FRONT_V(key[1], key[2]))
    if key[0] == "t":
        p, x = key[1:]
        if x in ("GV", "XA0", "XA1"):
            return s["tail_a"], TAIL_A(p, x)
        if x == "N":
            return s["tail_a"], TAIL_A(p, "N1")
        return s["tail_v"], TAIL_V(p, {"RY0": "YL0", "RY1": "YL1", "M": "M21"}.get(x, x))
    p, x = key[1:]
    return s["post_v"], POST_V(p, {"bonus": "bv", "mean": "d"}.get(x)) if x != "var" else 0


def rwkv_bank(b, *key):
    return b["ps"][:, RING[key] % 2]


def claim(pe, s, b, *key):
    i = RING[key]
    if i >= 2:
        before = RING_LIST[i - 2]
        if before[0] == "post" and before[2] == "var":
            pe.wait_ge(s["post_a"], POST_A(before[1], "sd"))
        else:
            pe.wait_ge(*freed_count(s, before))
    return b["ps"][:, i % 2]


def half(h):
    return slice(64 * h, 64 * h + 64)


def vhalf(h):
    return slice(64 - 64 * h, 128 - 64 * h)


def rwkv_gemm_pe(pe, s, b, ring, p, names):
    h = tiles_of(b["hh"], b["hl"])
    for x in names:
        w = ring.take(pe)
        if x != "L":
            ps = claim(pe, s, b, "g", p, x)
            split_matmuls(pe, ps, columns_of(w, KD), h, KD).then_inc(s["gemm_p"], 1)
            continue
        if p == 0:
            pe.wait_ge(s["lo_lo"], 3)
        for j, y, first, n in ((2, "g", 1, 2), (0, "w", 0, 1), (1, "a", 0, 1)):
            ps = claim(pe, s, b, "g", p, y)
            split_matmuls(pe, ps, columns_of(w, n, at=j * P), tiles_of(b["loh"][:, first:3], b["lol"][:, first:3]), n) \
                .then_inc(s["gemm_p"], 1)


def rwkv_ssq_pe(pe, s, b, p):
    ps = claim(pe, s, b, "ssq", p)
    pe.wait_ge(s["prep_a"], PREP_A(p, "sqk"))
    pe.matmul(ps, b["c"]("bd"), b["sqk"][:], start=True, stop=True).then_inc(s["ssq_p"], 1)


def rwkv_front_pe(pe, s, b, p):
    q = p % 2
    for x, src, step in (("trA", b["ar"][:, q, :, 0], "na"), ("trB", b["bh"], "bh"), ("trK", b["kh"], "kh"), ("trV", b["v"][:, q], None)):
        ps = claim(pe, s, b, "f", p, x)
        if step:
            pe.wait_ge(*((s["prep_v"], PREP_V(p, "na")) if step == "na" else (s["prep_g"], PREP_G(p, step))))
        for c in range(BLK):
            blk = src[:, c] if x == "trA" else src[:, c * P:(c + 1) * P]
            last = pe.transpose(ps[:, c * P:(c + 1) * P], blk, b["c"]("ident"))
        last.then_inc(s["front_p"], 1)
    pe.wait_ge(s["prep_v"], PREP_V(p, "rk"))
    for h in range(2):
        for m, left in enumerate((b["bt"], b["kt"])):
            for cc in range(2):
                i = 4 * h + 2 * m + cc
                ps = claim(pe, s, b, "f", p, f"T{i}")
                for c in (2 * cc, 2 * cc + 1):
                    last = pe.matmul(ps[:, (c % 2) * 256:(c % 2) * 256 + 256],
                                     left[half(h), c * P:(c + 1) * P], b["ar"][half(h), q, c].rearrange("p a t -> p (a t)"),
                                     start=True, stop=True)
                last.then_inc(s["front_p"], 1)


def rwkv_inv_pe(pe, s, b, p, between):
    def each(ps, lhs, rhs):
        for c in range(BLK):
            last = pe.matmul(ps[:, c * P:(c + 1) * P], lhs[:, c * P:(c + 1) * P], rhs(c), start=True, stop=True)
        last.then_inc(s["inv_p"], 1)

    for h in range(2):
        pe.wait_ge(s["inv_v"], INV_V(p, f"T0{h}"))
        each(b["ps"][:, 4 + h], b["XT"][:, h], lambda c: b["c"]("ident"))
    for l in range(1, LEVELS):
        for h in range(2):
            pe.wait_ge(s["inv_g"], INV_G(p, f"m{l}{h}"))
            if l > 1:
                pe.wait_ge(s["inv_v"], INV_V(p, f"X{l - 1}{h}"))
            else:
                pe.wait_ge(s["inv_a"], INV_A(p, f"X0{h}"))
            each(b["ps"][:, 2 + h], b["TM"][:, h, l % 2], lambda c: b["X"][:, h, c * P:(c + 1) * P])
        between(l)
        for h in range(2):
            pe.wait_ge(s["inv_a"], INV_A(p, f"W{l}{h}"))
            if l > 1:
                pe.wait_ge(s["inv_v"], INV_V(p, f"T{l - 1}{h}"))
            if l < 6:
                each(b["ps"][:, 4 + h], b["XT"][:, h], lambda c: b["Wm"][:, h, c])
            each(b["ps"][:, 6 + h], b["Wm"][:, h].rearrange("t c n -> t (c n)"), lambda c: b["XT"][:, h, c * P:(c + 1) * P])


def rwkv_tail_pe(pe, s, b, ring, p):
    def ahead(x):
        if p + 2 < PAIRS:
            rwkv_gemm_pe(pe, s, b, ring, p + 2, TAIL_GEMM[x])

    ps = claim(pe, s, b, "t", p, "GV")
    for h in range(2):
        for c in range(BLK):
            last = pe.matmul(ps[:, (2 * c + h) * 64:(2 * c + h) * 64 + 64], b["TK"][:, h, c, 0], b["Vt"][:, c, vhalf(h)],
                             start=True, stop=True)
    last.then_inc(s["tail_p"], 1)
    for h in range(2):
        ps = claim(pe, s, b, "t", p, f"XA{h}")
        if h == 0:
            pe.wait_ge(s["tail_a"], TAIL_A(p, "GV"))
        pe.wait_ge(s["inv_v"], INV_V(p, f"T6{h}"))
        for c in range(BLK):
            last = pe.matmul(ps[:, c * P:(c + 1) * P], b["XT"][:, h, c * P:(c + 1) * P], b["AG"][:, c, h], start=True, stop=True)
        last.then_inc(s["tail_p"], 1)
    for h in range(2):
        ps = claim(pe, s, b, "t", p, f"RY{h}")
        pe.wait_ge(s["tail_a"], TAIL_A(p, f"XA{h}"))
        for c in range(BLK):
            pc = ps[:, c * P:(c + 1) * P]
            pe.matmul(pc, b["Wm"][:, h, c], b["TB"][:, h, c, 1], start=True, stop=True)
            last = pe.matmul(pc[vhalf(h)], b["Vt"][:, c, vhalf(h)], b["TK"][:, h, c, 1], start=False, stop=True,
                             skip_group_check=True)
        last.then_inc(s["tail_p"], 1)
    ps = claim(pe, s, b, "t", p, "M")
    for h in range(2):
        for c in (1, 2):
            last = pe.matmul(ps[half(h), c * P + 64 * h:c * P + 64 * h + 64], b["Wm"][:, h, c, half(h)], b["Bt"][:, c, half(h)],
                             start=True, stop=True)
    last.then_inc(s["tail_p"], 1)
    ps = claim(pe, s, b, "t", p, "N")
    for h in range(2):
        for c in range(3):
            pc = ps[half(h), c * P + 64 - 64 * h:c * P + 128 - 64 * h]
            pe.matmul(pc, b["Bt"][:, c, half(h)], b["Wm"][:, h, c, vhalf(h)], start=True, stop=False)
            last = pe.matmul(pc, b["Kt"][:, c, half(h)], b["Vt"][:, c, vhalf(h)], start=False, stop=True)
    last.then_inc(s["tail_p"], 1)
    ahead("N")
    for c, x in ((1, "S2"), (2, "S3")):
        ps = claim(pe, s, b, "t", p, x)
        if c == 1:
            pe.wait_ge(s["tail_a"], TAIL_A(p, "N1"))
            pe.wait_ge(s["tail_v"], TAIL_V(p, "M21"))
        else:
            pe.wait_ge(s["tail_v"], TAIL_V(p, "S2"))
        pe.matmul(ps[:, 0:P], b["M"][:, c], b["N"][:, c - 1], start=True, stop=True).then_inc(s["tail_p"], 1)
        if c == 1:
            ahead("S2")
    ps = claim(pe, s, b, "t", p, "Y")
    pe.wait_ge(s["tail_v"], TAIL_V(p, "S3"))
    for c in (1, 2, 3):
        last = pe.matmul(ps[:, c * P:(c + 1) * P], b["N"][:, c - 1], b["RY"][:, c * P:(c + 1) * P], start=True, stop=True)
    last.then_inc(s["tail_p"], 1)


def rwkv_post_pe(pe, s, b, p):
    q = p % 2
    ps = claim(pe, s, b, "post", p, "bonus")
    pe.matmul(ps, b["c"]("bdswap"), b["rk"][:, q], start=True, stop=True).then_inc(s["post_p"], 1)
    ps = claim(pe, s, b, "post", p, "mean")
    pe.wait_ge(s["tail_v"], TAIL_V(p, "Y"))
    pe.matmul(ps, b["c"]("bd"), b["y"][:], start=True, stop=True).then_inc(s["post_p"], 1)


def rwkv_var_pe(pe, s, b, p):
    ps = claim(pe, s, b, "post", p, "var")
    pe.wait_ge(s["post_a"], POST_A(p, "sq"))
    pe.matmul(ps, b["c"]("bd"), b["ysq"][:], start=True, stop=True).then_inc(s["post_p"], 1)


def rwkv_ev_act(act, s, b, high, p, names):
    for x in names:
        j = "rkvL".index(x)
        high.around(act, 3 + 4 * p + j)
        if x != "L":
            act.wait_ge(s["gemm_p"], GEMM(p, x))
            if p:
                act.wait_ge(s["mix"], MIX(p - 1, x))
            if x == "r" and p >= 3:
                act.wait_ge(s["post_v"], POST_V(p - 3, "yl"))
            act.activation(b["zp"][:, j, 1:TOK + 1], rwkv_bank(b, "g", p, x), ACT.Copy).then_inc(s["gemm_ev"], 1)
            continue
        act.wait_ge(s["gemm_p"], GEMM(p, "g"))
        act.activation(b["gS"][:, p % 3], rwkv_bank(b, "g", p, "g"), ACT.Copy).then_inc(s["gemm_ev"], 1)
        for y, dst, bias in (("w", b["wS"], "w0"), ("a", b["aS"], "a0")):
            act.wait_ge(s["gemm_p"], GEMM(p, y))
            if p:
                act.wait_ge(s["prep_v"], PREP_V(p - 1, "kf"))
            act.activation(dst[:], rwkv_bank(b, "g", p, y), ACT.Sigmoid, bias=b["p"](bias, p)).then_inc(s["gemm_ev"], 1)


def rwkv_prep_act(act, s, b, p):
    act.wait_ge(s["prep_v"], PREP_V(p, "kkr"))
    if p:
        act.wait_ge(s["ssq_p"], p)
        act.wait_ge(s["prep_g"], PREP_G(p - 1, "kh"))
    act.activation(b["sqk"][:], b["kkr"][:], ACT.Square).then_inc(s["prep_a"], 1)
    for dst, src, k in ((b["en"], b["cm"], DECAY), (b["cm"], b["cm"], -DECAY), (b["cum"], b["cum"], -DECAY)):
        act.activation(dst[:], src[:], ACT.Exp, scale=k).then_inc(s["prep_a"], 1)
    act.activation(b["f"][:, p % 2], b["fe"][:], ACT.Exp, scale=-DECAY).then_inc(s["prep_a"], 1)


def rwkv_root_act(act, s, b, p):
    act.wait_ge(s["ssq_p"], p + 1)
    act.activation(b["sqk"][:], rwkv_bank(b, "ssq", p), ACT.Sqrt).then_inc(s["prep_a"], 1)


def rwkv_front_act(act, s, b, p):
    act.wait_ge(s["front_p"], FRONT_P(p, "trA"))
    if p:
        act.wait_ge(s["tail_p"], TAIL_P(p - 1, "Y"))
    ps = rwkv_bank(b, "f", p, "trA").rearrange("t (c h n) -> t c h n", c=BLK, h=2)
    ag = b["AG"][:].rearrange("t c h n -> t c (h n)").rearrange("t c (x n) -> t c x n", n=64)[:, :, 0:4:3]
    act.activation(ag, ps, ACT.Copy).then_inc(s["front_a"], 1)
    for x, dst in (("trB", b["Bt"]), ("trK", b["Kt"]), ("trV", b["Vt"])):
        act.wait_ge(s["front_p"], FRONT_P(p, x))
        act.activation(dst[:].rearrange("t c n -> t (c n)"), rwkv_bank(b, "f", p, x), ACT.Copy).then_inc(s["front_a"], 1)


def rwkv_inv_act(act, s, b, p, between):
    for h in range(2):
        act.wait_ge(s["inv_p"], INV_P(p, f"X0{h}"))
        act.activation(b["X"][:, h], b["ps"][:, 4 + h], ACT.Copy).then_inc(s["inv_a"], 1)
    for l in range(1, LEVELS):
        for h in range(2):
            act.wait_ge(s["inv_p"], INV_P(p, f"W{l}{h}"))
            if l > 1:
                act.wait_ge(s["inv_p"], INV_P(p, f"T{l - 1}{h}"))
            act.activation(b["Wm"][:, h].rearrange("t c n -> t (c n)"), b["ps"][:, 2 + h], ACT.Copy).then_inc(s["inv_a"], 1)
        between(l)


def rwkv_tail_act(act, s, b, high, p):
    act.wait_ge(s["tail_p"], TAIL_P(p, "GV"))
    gv = b["AG"][:].rearrange("t c h n -> t c (h n)").rearrange("t c (x n) -> t c x n", n=64)[:, :, 1:3]
    act.activation(gv, rwkv_bank(b, "t", p, "GV").rearrange("t (c h n) -> t c h n", c=BLK, h=2),
                   ACT.Copy).then_inc(s["tail_a"], 1)
    for h in range(2):
        act.wait_ge(s["tail_p"], TAIL_P(p, f"XA{h}"))
        act.activation(b["Wm"][:, h].rearrange("t c n -> t (c n)"), rwkv_bank(b, "t", p, f"XA{h}"), ACT.Copy) \
            .then_inc(s["tail_a"], 1)
    act.wait_ge(s["tail_p"], TAIL_P(p, "N"))
    for h in range(2):
        ps = rwkv_bank(b, "t", p, "N").rearrange("k (c v) -> k c v", v=P)
        act.activation(b["N"][half(h), 0:3, vhalf(h)], ps[half(h), 0:3, vhalf(h)], ACT.Copy).then_inc(s["tail_a"], 1)
    if p + 2 < PAIRS:
        rwkv_ev_act(act, s, b, high, p + 2, "rk")


def rwkv_post_act(act, s, b, p):
    act.wait_ge(s["post_v"], POST_V(p, "d"))
    act.activation(b["ysq"][:], b["dd"][:], ACT.Square).then_inc(s["post_a"], 1)


def rwkv_root2_act(act, s, b, p):
    act.wait_ge(s["post_p"], POST_P(p, "var"))
    act.activation(b["ysq"][:], rwkv_bank(b, "post", p, "var"), ACT.Sqrt, scale=1.0 / 64, bias=b["c"]("epsgn")) \
        .then_inc(s["post_a"], 1)


def rwkv_mix_dve(dve, s, b, p, names="rkv"):
    dst = {"r": b["r"][:], "k": b["k"][:], "v": b["v"][:, p % 2]}
    for x in names:
        j = "rkv".index(x)
        dve.wait_ge(s["gemm_ev"], EV(p, x))
        if p and j < 2:
            dve.wait_ge(s["prep_g"], PREP_G(p - 1, ("bt", "kt")[j]))
        dve.tensor_tensor(b["dz"][:, j], b["zp"][:, j, 0:TOK], b["zp"][:, j, 1:TOK + 1], SUB).then_inc(s["mix"], 1)
        dve.wait_ge(s["mix"], MIX(p, "d" + x))
        dve.scalar_tensor_tensor(out=dst[x], in0=b["dz"][:, j], scalar=b["p"]("mu", 3 + 8 * j + p),
                                 in1=b["zp"][:, j, 1:TOK + 1], op0=MUL, op1=ADD).then_inc(s["mix"], 1)


def chunks(ap):
    return ap.rearrange("p (c t) -> p c t", t=P)


def spread(col):
    return col.broadcast_to([P, BLK, P])


def rwkv_prep1_dve(dve, s, b, p):
    q = p % 2
    done = lambda x: dve.wait_ge(s["prep_v"], PREP_V(p, x))
    dve.wait_ge(s["gemm_ev"], EV(p, "w"))
    for c in range(BLK):
        dve.tensor_tensor_scan(out=b["cum"][:, c * P:(c + 1) * P], data0=b["c"]("ones"), data1=b["wS"][:, c * P:(c + 1) * P],
                               initial=0.0, op0=MUL, op1=ADD).then_inc(s["prep_v"], 1)
    done("c3")
    cum = chunks(b["cum"][:])
    if p:
        dve.wait_ge(s["prep_a"], PREP_A(p - 1, "f"))
    dve.tensor_tensor(chunks(b["cm"][:]), cum, spread(cum[:, :, 63:64]), SUB).then_inc(s["prep_v"], 1)
    done("cm")
    dve.tensor_tensor(b["fe"][:, 0:3], chunks(b["cm"][:])[:, 0:3, 127], cum[:, 1:4, 63], ADD).then_inc(s["prep_v"], 1)
    done("fe")
    dve.tensor_tensor(b["cum"][:], b["cm"][:], b["wS"][:], SUB).then_inc(s["prep_v"], 1)
    dve.wait_ge(s["mix"], MIX(p, "k"))
    dve.tensor_scalar(b["kkr"][:], b["k"][:], b["p"]("kk", p), None, MUL).then_inc(s["prep_v"], 1)


def rwkv_prep2_dve(dve, s, b, p):
    done = lambda x: dve.wait_ge(s["prep_v"], PREP_V(p, x))
    dve.wait_ge(s["prep_a"], PREP_A(p, "rt"))
    dve.tensor_scalar(b["sqk"][:], b["sqk"][:], 1e-12, None, MAX).then_inc(s["prep_v"], 1)
    done("big")
    dve.reciprocal(b["sqk"][:], b["sqk"][:]).then_inc(s["prep_v"], 1)


def rwkv_prep2b_dve(dve, s, b, p):
    q = p % 2
    done = lambda x: dve.wait_ge(s["prep_v"], PREP_V(p, x))
    done("rn")
    dve.tensor_tensor(b["kkr"][:], b["kkr"][:], b["sqk"][:], MUL).then_inc(s["prep_v"], 1)
    done("kk")
    dve.scalar_tensor_tensor(out=b["ar"][:, q, :, 0], in0=chunks(b["kkr"][:]), scalar=-1.0, in1=chunks(b["cum"][:]),
                             op0=MUL, op1=MUL).then_inc(s["prep_v"], 1)
    dve.tensor_tensor(b["ar"][:, q, :, 1], chunks(b["r"][:]), chunks(b["cm"][:]), MUL).then_inc(s["prep_v"], 1)
    dve.tensor_tensor(b["dz"][:, 0], b["kkr"][:], b["aS"][:], MUL).then_inc(s["prep_v"], 1)
    done("b")


def rwkv_prep_pool(pool, s, b, p, names="bk"):
    f = spread(b["f"][:, p % 2, :, None])
    if p:
        pool.wait_ge(s["front_p"], FRONT_P(p - 1, "T7"))
    for x, src, made, t, th in (("b", 0, "b", b["bt"], b["bh"]), ("k", 1, "ks", b["kt"], b["kh"])):
        if x not in names:
            continue
        pool.wait_ge(s["prep_v"], PREP_V(p, made))
        pool.wait_ge(s["prep_a"], PREP_A(p, "f"))
        pool.tensor_tensor(t[:], b["dz"][:, src], b["en"][:], MUL).then_inc(s["prep_g"], 1)
        pool.wait_ge(s["prep_g"], PREP_G(p, x + "t"))
        pool.tensor_tensor(chunks(th[:]), chunks(t[:]), f, MUL).then_inc(s["prep_g"], 1)


def rwkv_prep3_dve(dve, s, b, p):
    q = p % 2
    done = lambda x: dve.wait_ge(s["prep_v"], PREP_V(p, x))
    dve.tensor_scalar(b["dz"][:, 1], b["aS"][:], -1.0, b["p"]("ka", p), ADD, MUL).then_inc(s["prep_v"], 1)
    done("kf")
    dve.scalar_tensor_tensor(out=b["dz"][:, 1], in0=b["dz"][:, 1], scalar=1.0, in1=b["k"][:], op0=ADD, op1=MUL) \
        .then_inc(s["prep_v"], 1)
    done("ks")
    dve.scalar_tensor_tensor(out=b["rk"][:, q], in0=b["r"][:], scalar=b["p"]("rk", p), in1=b["dz"][:, 1], op0=MUL, op1=MUL) \
        .then_inc(s["prep_v"], 1)


def rwkv_front_dve(dve, s, b, p):
    mask = b["c"]("tmask").rearrange("j (x t) -> j x t", x=1).broadcast_to([P, 2, 256])
    if p:
        dve.wait_ge(s["tail_p"], TAIL_P(p - 1, "Y"))
    for i in range(8):
        h, m, cc = i // 4, i // 2 % 2, i % 2
        dve.wait_ge(s["front_p"], FRONT_P(p, f"T{i}"))
        dst = (b["TB"], b["TK"])[m][:, h, 2 * cc:2 * cc + 2].rearrange("j c a t -> j c (a t)")
        dve.tensor_tensor(dst, rwkv_bank(b, "f", p, f"T{i}").rearrange("j (c x) -> j c x", c=2), mask, MUL) \
            .then_inc(s["front_v"], 1)


def rwkv_inv_pool(pool, s, b, p, between):
    for l in range(LEVELS):
        for h in range(2):
            if l == 0:
                pool.wait_ge(s["front_v"], FRONT_V(p, f"T{4 * h + 1}"))
            else:
                if l >= 2:
                    pool.wait_ge(s["inv_p"], INV_P(p, f"W{l - 2}{h}") if l > 2 else INV_P(p, f"X0{h}"))
            mask = b["c"]("lvl").rearrange("j (l x t) -> j l x t", l=LEVELS, x=1)[:, l].broadcast_to([P, BLK, P])
            pool.tensor_tensor(chunks(b["TM"][:, h, l % 2]), b["TB"][:, h, :, 0], mask, MUL).then_inc(s["inv_g"], 1)
        between(l)


def rwkv_inv_dve(dve, s, b, p, between):
    ident = b["c"]("ident").rearrange("j (x t) -> j x t", x=1).broadcast_to([P, BLK, P])
    for h in range(2):
        dve.wait_ge(s["inv_g"], INV_G(p, f"m0{h}"))
        dve.tensor_tensor(chunks(b["XT"][:, h]), chunks(b["TM"][:, h, 0]), ident, ADD).then_inc(s["inv_v"], 1)
    between(0)
    for l in range(1, LEVELS):
        for h in range(2):
            if l < 6:
                dve.wait_ge(s["inv_p"], INV_P(p, f"X{l}{h}"))
                dve.tensor_tensor(b["X"][:, h], b["X"][:, h], b["ps"][:, 4 + h], ADD).then_inc(s["inv_v"], 1)
            dve.wait_ge(s["inv_p"], INV_P(p, f"T{l}{h}"))
            dve.tensor_tensor(b["XT"][:, h], b["XT"][:, h], b["ps"][:, 6 + h], ADD).then_inc(s["inv_v"], 1)
        between(l)


def rwkv_tail_dve(dve, s, b, p):
    q = p % 2
    for h in range(2):
        dve.wait_ge(s["tail_p"], TAIL_P(p, f"RY{h}"))
        ps = rwkv_bank(b, "t", p, f"RY{h}")
        dve.tensor_tensor(chunks(b["RY"][half(h)]), chunks(ps[half(h)]), b["ar"][half(h), q, :, 1], ADD).then_inc(s["tail_v"], 1)
        if h == 0 and p >= 2:
            dve.wait_ge(s["post_v"], POST_V(p - 2, "d"))
        dve.tensor_copy(b["y"][vhalf(h)], ps[vhalf(h)]).then_inc(s["tail_v"], 1)
    dve.wait_ge(s["tail_p"], TAIL_P(p, "M"))
    ps = rwkv_bank(b, "t", p, "M")
    for c in (1, 2):
        for h in range(2):
            cols = slice(c * P + 64 * h, c * P + 64 * h + 64)
            dve.scalar_tensor_tensor(out=b["M"][half(h), c, half(h)], in0=b["c"]("ident")[half(h), half(h)],
                                     scalar=b["f"][half(h), q, c:c + 1], in1=ps[half(h), cols], op0=MUL, op1=ADD) \
                .then_inc(s["tail_v"], 1)
    for c, x in ((1, "S2"), (2, "S3")):
        dve.wait_ge(s["tail_p"], TAIL_P(p, x))
        dve.tensor_tensor(b["N"][:, c], b["N"][:, c], rwkv_bank(b, "t", p, x)[:, 0:P], ADD).then_inc(s["tail_v"], 1)
    dve.wait_ge(s["tail_p"], TAIL_P(p, "Y"))
    dve.tensor_tensor(b["y"][:, P:TOK], b["y"][:, P:TOK], rwkv_bank(b, "t", p, "Y")[:, P:TOK], ADD).then_inc(s["tail_v"], 1)


def rwkv_post_dve(dve, s, b, p):
    dve.wait_ge(s["post_p"], POST_P(p, "bonus"))
    dve.tensor_tensor(b["rk"][:, p % 2], rwkv_bank(b, "post", p, "bonus"), b["v"][:, p % 2], MUL).then_inc(s["post_v"], 1)
    dve.wait_ge(s["post_p"], POST_P(p, "mean"))
    dve.scalar_tensor_tensor(out=b["dd"][:], in0=rwkv_bank(b, "post", p, "mean"), scalar=-1.0 / 64, in1=b["y"][:],
                             op0=MUL, op1=ADD).then_inc(s["post_v"], 1)


def rwkv_out_dve(dve, s, b, p):
    done = lambda x: dve.wait_ge(s["post_v"], POST_V(p, x))
    dve.wait_ge(s["post_a"], POST_A(p, "sd"))
    dve.reciprocal(b["ysq"][:], b["ysq"][:]).then_inc(s["post_v"], 1)
    done("rr")
    dve.tensor_tensor(b["dd"][:], b["dd"][:], b["ysq"][:], MUL).then_inc(s["post_v"], 1)


def rwkv_out2_dve(dve, s, b, p):
    q = p % 2
    done = lambda x: dve.wait_ge(s["post_v"], POST_V(p, x))
    done("yn")
    dve.tensor_scalar(b["dd"][:], b["dd"][:], b["p"]("gnw", p), b["p"]("gnb", p), MUL, ADD).then_inc(s["post_v"], 1)
    done("ya")
    dve.tensor_tensor(b["dd"][:], b["dd"][:], b["rk"][:, q], ADD).then_inc(s["post_v"], 1)
    done("o")
    dve.tensor_tensor(b["dd"][:], b["dd"][:], b["gS"][:, p % 3], MUL).then_inc(s["post_v"], 1)
    done("og")
    if p:
        dve.wait_ge(s["y_out"], 32 * p)
    dve.tensor_copy(b["yh"][:], b["dd"][:]).then_inc(s["post_v"], 1)
    done("yh")
    dve.tensor_tensor(b["yl"][:], b["dd"][:], b["yh"][:].bitcast(F32), SUB).then_inc(s["post_v"], 1)


def rwkv_store_act(act, s, b, p):
    act.wait_ge(s["post_v"], POST_V(p, "yl"))
    act.dma_start(b["park_yh"][p], b["yh"][:].bitcast(F32)).then_inc(s["y_out"], 16)
    act.dma_start(b["park_yl"][p], b["yl"][:].bitcast(F32)).then_inc(s["y_out"], 16)


def rwkv_pe(pe, s, b, ring):
    for i in range(3):
        w = ring.take(pe)
        ps = claim(pe, s, b, "lo", i)
        for k in range(KD):
            if i == 0:
                pe.wait_ge(s["h1_lo"], k + 1)
            last = split_matmuls(pe, ps, columns_of(w, 1, at=k * P), tiles_of(b["hh"][:, k:k + 1], b["hl"][:, k:k + 1]), 1,
                                 start=k == 0, stop=k == KD - 1)
        last.then_inc(s["lo_mm"], 1)
    rwkv_gemm_pe(pe, s, b, ring, 0, "rkvL")
    rwkv_ssq_pe(pe, s, b, 0)
    rwkv_gemm_pe(pe, s, b, ring, 1, "rk")
    for p in range(PAIRS):
        rwkv_front_pe(pe, s, b, p)
        if p + 1 < PAIRS:
            rwkv_gemm_pe(pe, s, b, ring, p + 1, "vL")

        def between(l):
            if l == 2 and p:
                rwkv_post_pe(pe, s, b, p - 1)
            if l == 3:
                if p + 1 < PAIRS:
                    rwkv_ssq_pe(pe, s, b, p + 1)
                if p:
                    rwkv_var_pe(pe, s, b, p - 1)
        rwkv_inv_pe(pe, s, b, p, between)
        rwkv_tail_pe(pe, s, b, ring, p)
    rwkv_post_pe(pe, s, b, PAIRS - 1)
    rwkv_var_pe(pe, s, b, PAIRS - 1)


def rwkv_act(act, s, b, high):
    for i in range(3):
        high.around(act, i)
        act.wait_ge(s["lo_mm"], i + 1)
        act.activation(b["zp"][:, i, 1:TOK + 1], b["ps"][:, i % 2], ACT.Copy).then_inc(s["lo_z"], 1)
    act.wait_ge(s["lo_mix"], 3)
    act.activation(b["lo"][0:64, 0], b["lo"][0:64, 0], ACT.Tanh).then_inc(s["lo_act"], 1)
    act.activation(b["lo"][:, 1], b["lo"][:, 1], ACT.Sigmoid).then_inc(s["lo_act"], 1)
    act.activation(b["lo"][:, 2], b["lo"][:, 2], ACT.Sigmoid).then_inc(s["lo_act"], 1)
    for i in range(3):
        act.wait_ge(s["lo_act"], i + 1)
        act.activation(b["loh"][:, i], b["lo"][:, i], ACT.Copy).then_inc(s["lo_hi"], 1)
    rwkv_ev_act(act, s, b, high, 0, "rkvL")
    rwkv_prep_act(act, s, b, 0)
    rwkv_root_act(act, s, b, 0)
    rwkv_ev_act(act, s, b, high, 1, "rk")
    for p in range(PAIRS):
        rwkv_front_act(act, s, b, p)
        if p + 1 < PAIRS:
            rwkv_ev_act(act, s, b, high, p + 1, "vL")

        def between(l):
            if l == 2:
                if p + 1 < PAIRS:
                    rwkv_prep_act(act, s, b, p + 1)
                if p:
                    rwkv_post_act(act, s, b, p - 1)
            if l == 3:
                if p + 1 < PAIRS:
                    rwkv_root_act(act, s, b, p + 1)
                if p:
                    rwkv_root2_act(act, s, b, p - 1)
        rwkv_inv_act(act, s, b, p, between)
        rwkv_tail_act(act, s, b, high, p)
        if p:
            rwkv_store_act(act, s, b, p - 1)
    rwkv_post_act(act, s, b, PAIRS - 1)
    rwkv_root2_act(act, s, b, PAIRS - 1)
    rwkv_store_act(act, s, b, PAIRS - 1)


def rwkv_dve(dve, s, b):
    for i in range(3):
        dve.wait_ge(s["lo_z"], i + 1)
        dve.tensor_tensor(b["dz"][:, i], b["zp"][:, i, 0:TOK], b["zp"][:, i, 1:TOK + 1], SUB).then_inc(s["lo_d"], 1)
        dve.wait_ge(s["lo_d"], i + 1)
        dve.scalar_tensor_tensor(out=b["lo"][:, i], in0=b["dz"][:, i], scalar=b["p"]("mu", i),
                                 in1=b["zp"][:, i, 1:TOK + 1], op0=MUL, op1=ADD).then_inc(s["lo_mix"], 1)
    for i in range(3):
        dve.wait_ge(s["lo_hi"], i + 1)
        dve.tensor_tensor(b["lol"][:, i], b["lo"][:, i], b["loh"][:, i].bitcast(F32), SUB).then_inc(s["lo_lo"], 1)
    rwkv_mix_dve(dve, s, b, 0)
    rwkv_prep1_dve(dve, s, b, 0)
    rwkv_prep2_dve(dve, s, b, 0)
    rwkv_prep2b_dve(dve, s, b, 0)
    rwkv_prep3_dve(dve, s, b, 0)
    for p in range(PAIRS):
        rwkv_front_dve(dve, s, b, p)

        def between(l):
            if p + 1 < PAIRS:
                if l == 0:
                    rwkv_mix_dve(dve, s, b, p + 1, "rk")
                if l == 1:
                    rwkv_prep1_dve(dve, s, b, p + 1)
                if l == 3:
                    rwkv_prep2_dve(dve, s, b, p + 1)
                if l == 4:
                    rwkv_prep2b_dve(dve, s, b, p + 1)
            if l == 2:
                if p:
                    rwkv_post_dve(dve, s, b, p - 1)
                if p + 1 < PAIRS:
                    rwkv_mix_dve(dve, s, b, p + 1, "v")
            if l == 5 and p:
                rwkv_out_dve(dve, s, b, p - 1)
            if l == 6:
                if p:
                    rwkv_out2_dve(dve, s, b, p - 1)
                if p + 1 < PAIRS:
                    rwkv_prep3_dve(dve, s, b, p + 1)
        rwkv_inv_dve(dve, s, b, p, between)
        rwkv_tail_dve(dve, s, b, p)
    rwkv_post_dve(dve, s, b, PAIRS - 1)
    rwkv_out_dve(dve, s, b, PAIRS - 1)
    rwkv_out2_dve(dve, s, b, PAIRS - 1)


def rwkv_pool(pool, s, b):
    low_parts(pool, s, b, 0, 3 + 6)
    rwkv_prep_pool(pool, s, b, 0)
    low_parts(pool, s, b, 3 + 6, 3 + 8)
    for p in range(PAIRS):
        def between(l):
            if p + 1 < PAIRS and l in (5, 6):
                rwkv_prep_pool(pool, s, b, p + 1, "b" if l == 5 else "k")
            if p + 2 < PAIRS and l in (2, 6):
                u = 3 + 4 * (p + 2) + (0 if l == 2 else 2)
                low_parts(pool, s, b, u, u + 2)
        rwkv_inv_pool(pool, s, b, p, between)


def rwkv_buffers(ctx, nc, b):
    def sb(name, *shape, dt=F32):
        b[name] = ctx.enter_context(nc.sbuf_tensor(name, [P, *shape], dt))
    for name in ("v", "rk"):
        sb(name, 2, TOK)
    sb("gS", 3, TOK)
    sb("zp", 3, TOK + 1)
    sb("dz", 3, TOK)
    sb("loh", 3, TOK, dt=F32R)
    sb("lol", 3, TOK, dt=F32R)
    for name in ("r", "k", "wS", "aS", "y", "cum", "cm", "en", "kkr", "sqk", "bt", "bh", "kt", "kh"):
        sb(name, TOK)
    sb("yh", TOK, dt=F32R)
    sb("yl", TOK, dt=F32R)
    sb("fe", BLK)
    sb("f", 2, BLK)
    sb("ar", 2, BLK, 2, P)
    for name in ("Bt", "Kt", "Vt"):
        sb(name, BLK, P)
    sb("AG", BLK, 2, P)
    sb("TB", 2, BLK, 2, P)
    sb("TK", 2, BLK, 2, P)
    sb("Wm", 2, BLK, P)
    sb("M", 3, P)
    sb("N", 3, P)
    b["ysq"], b["dd"] = b["zp"][:, 0, 1:TOK + 1], b["zp"][:, 1, 1:TOK + 1]
    b["RY"] = b["sqk"]
    b["lo"] = b["ar"][:].rearrange("p q c a t -> p (q c a t)").rearrange("p (i t) -> p i t", t=TOK)


ROPE_V = Steps("t1", "t2", "q")
SOFT_V = Steps("m0", *[f"a{n}{h}" for n in range(4) for h in range(2)], "mx", "ml", "ng", "sk")
NORMP_V = Steps("den", "rd", "pn")
SOFT_A = Steps(*[f"e{i}" for i in range(8)], "es")
ATT_SEMS = ["ao_hi", "ao_lo", "y_back", "qkv_p", "q_z", "v_z", "perm_p", "rope_v", "score_p", "soft_v", "soft_a", "tr_p", "pt_a", "pv_p", "normp_v"]


def attention_pe(pe, s, b, ring):
    h = tiles_of(b["hh"], b["hl"])
    for i in range(11):
        if i < 10:
            w = ring.take(pe)
            if i >= 4:
                pe.wait_ge(s["q_z"], i - 3)
            split_matmuls(pe, b["ps"][:, i % 4], columns_of(w, KD), h, KD).then_inc(s["qkv_p"], 1)
        if i >= 1:
            pe.wait_ge(s["q_z"], i)
            if i >= 3:
                pe.wait_ge(s["rope_v"], ROPE_V(i - 3, "t2"))
            pe.matmul(b["ps"][:, 4 + (i - 1) % 2], b["c"]("perm1"), b["zr"][:, (i - 1) % 2], start=True, stop=True) \
                .then_inc(s["perm_p"], 1)
    pe.wait_ge(s["q_z"], 10)
    for u in range(2):
        w = ring.take(pe)
        for t in range(BLK):
            left = [lambda k, x=x: x[:, k, t * P:(t + 1) * P] for x in (b["hh"], b["hl"])]
            split_matmuls(pe, b["ps"][:, t, u * P:(u + 1) * P], left, columns_of(w, KD), KD).then_inc(s["qkv_p"], 1)
    pe.wait_ge(s["rope_v"], ROPE_V(9, "q"))
    pe.wait_ge(s["v_z"], 4)

    def scores(m):
        for nn in range(2):
            for h in range(2):
                if m:
                    pe.wait_ge(s["soft_v"], SOFT_V(m - 1, f"a{2 * nn + 1}{h}"))
                for n in (2 * nn, 2 * nn + 1):
                    lo = 0 if n else P
                    last = pe.matmul(b["ps"][:, 2 * h + nn, n % 2 * 256 + lo:n % 2 * 256 + 256],
                                     b["qk"][half(h), m, n * P:(n + 1) * P],
                                     b["qk"][half(h), 8 + m // 4, (n - 1) * P + lo:(n + 1) * P], start=True, stop=True)
                last.then_inc(s["score_p"], 1)

    scores(0)
    scores(1)
    for m in range(PAIRS):
        if m + 2 < PAIRS:
            scores(m + 2)
        pe.wait_ge(s["normp_v"], NORMP_V(m, "pn"))
        for n in range(BLK):
            if n >= 2 or m:
                pe.wait_ge(s["pt_a"], 4 * m + n - 1)
            for h in range(2):
                for kb in range(2):
                    if n or kb:
                        last = pe.transpose(b["ps"][:, 4 + n % 2, (2 * h + kb) * P:(2 * h + kb + 1) * P],
                                            b["sm"][:, m % 3, 2 * n + h, kb * P:(kb + 1) * P], b["c"]("ident"))
            last.then_inc(s["tr_p"], 1)
        if m >= 2:
            pe.wait_ge(s["ao_lo"], m - 1)
        for n in range(BLK):
            pe.wait_ge(s["pt_a"], 4 * m + n + 1)
            for h in range(2):
                kbs = (0, 1) if n else (1,)
                for kb in kbs:
                    kv = 2 * (m // 4) + h
                    last = pe.matmul(b["ps"][half(h), 6 + m % 2, n * P:(n + 1) * P],
                                     b["vtok"][:, n - 1 + kb, kv * HD:(kv + 1) * HD], b["PT"][:, n, 2 * h + kb],
                                     start=kb == kbs[0], stop=kb == 1)
        last.then_inc(s["pv_p"], 1)


def attention_act(act, s, b, high):
    for i in range(10):
        high.around(act, 35 + i)
        act.wait_ge(s["qkv_p"], i + 1)
        if i >= 2:
            act.wait_ge(s["perm_p"], i - 1)
            act.wait_ge(s["rope_v"], ROPE_V(i - 2, "t1"))
        if i == 0:
            act.wait_ge(s["y_out"], 32 * PAIRS)
        act.activation(b["zr"][:, i % 2], b["ps"][:, i % 4], ACT.Copy).then_inc(s["q_z"], 1)
    for u in (45, 46):
        high.around(act, u)
    for t in range(BLK):
        act.wait_ge(s["qkv_p"], 15 + t)
        act.activation(b["vtok"][:, t], b["ps"][:, t, 0:256], ACT.Copy).then_inc(s["v_z"], 1)

    def exps(m):
        act.wait_ge(s["soft_v"], SOFT_V(m, "ng"))
        if m >= 2:
            act.wait_ge(s["normp_v"], NORMP_V(m - 2, "den"))
        for i in range(8):
            act.activation(b["sm"][:, m % 3, i], b["sm"][:, m % 3, i], ACT.Exp, scale=HD ** -0.5, bias=b["ng"][:, m % 2, i:i + 1],
                           accum_out=b["sum"][:, m % 2, i:i + 1]).then_inc(s["soft_a"], 1)
        act.wait_ge(s["soft_v"], SOFT_V(m, "sk"))
        act.activation(b["sk"][:, m % 2], b["sk"][:, m % 2], ACT.Exp).then_inc(s["soft_a"], 1)

    def out_high(m):
        act.wait_ge(s["pv_p"], m + 1)
        act.activation(b["aoh"][:, m], b["ps"][:, 6 + m % 2], ACT.Copy).then_inc(s["ao_hi"], 1)

    exps(0)
    for m in range(PAIRS):
        if m + 1 < PAIRS:
            exps(m + 1)
        if m:
            out_high(m - 1)
        for n in range(BLK):
            act.wait_ge(s["tr_p"], 4 * m + n + 1)
            if m:
                act.wait_ge(s["pv_p"], m)
            ps = b["ps"][:, 4 + n % 2].rearrange("k (x q) -> k x q", q=P)
            if n:
                act.activation(b["PT"][:, n], ps, ACT.Copy).then_inc(s["pt_a"], 1)
            else:
                act.activation(b["PT"][:, n, 1:4:2], ps[:, 1:4:2], ACT.Copy).then_inc(s["pt_a"], 1)
    out_high(PAIRS - 1)
    act.wait_ge(s["normp_v"], NORMP_V(PAIRS - 1, "pn"))
    for p in range(PAIRS):
        act.dma_start(b["yrh"][:, p].bitcast(F32), b["park_yh"][p]).then_inc(s["y_back"], 16)
        act.dma_start(b["yrl"][:, p].bitcast(F32), b["park_yl"][p]).then_inc(s["y_back"], 16)


def attention_dve(dve, s, b):
    for i in range(10):
        dve.wait_ge(s["q_z"], i + 1)
        if i >= 2:
            dve.wait_ge(s["rope_v"], ROPE_V(i - 2, "q"))
        dve.tensor_tensor(b["t1"][:, i % 2], b["zr"][:, i % 2], b["cos"][:], MUL).then_inc(s["rope_v"], 1)
        dve.wait_ge(s["perm_p"], i + 1)
        dve.tensor_tensor(b["t2"][:, i % 2], b["ps"][:, 4 + i % 2], b["sin"][:], MUL).then_inc(s["rope_v"], 1)
        dve.wait_ge(s["rope_v"], ROPE_V(i, "t2"))
        dve.tensor_tensor(b["qk"][:, i], b["t1"][:, i % 2], b["t2"][:, i % 2], ADD).then_inc(s["rope_v"], 1)
    mask = b["c"]("amask")

    def soft(m):
        q = m % 2
        done = lambda x: dve.wait_ge(s["soft_v"], SOFT_V(m, x))
        if m >= 3:
            dve.wait_ge(s["tr_p"], 4 * (m - 2))
        dve.memset(b["sm"][:, m % 3, 0:2, 0:P], NEG).then_inc(s["soft_v"], 1)
        for n in range(BLK):
            for h in range(2):
                dve.wait_ge(s["score_p"], 4 * m + 2 * (n // 2) + h + 1)
                lo = 0 if n else P
                dve.tensor_tensor(b["sm"][:, m % 3, 2 * n + h, lo:256], b["ps"][:, 2 * h + n // 2, n % 2 * 256 + lo:n % 2 * 256 + 256],
                                  mask[:, lo:256], ADD).then_inc(s["soft_v"], 1)
        done("a31")
        dve.tensor_reduce(b["mx"][:, q], b["sm"][:, m % 3], AX.X, MAX).then_inc(s["soft_v"], 1)
        done("mx")
        sink = b["par"][:, PAR1["sink"] + 8 * m:PAR1["sink"] + 8 * m + 8]
        dve.scalar_tensor_tensor(out=b["mx"][:, q], in0=b["mx"][:, q], scalar=HD ** -0.5, in1=sink, op0=MUL, op1=MAX) \
            .then_inc(s["soft_v"], 1)
        done("ml")
        dve.tensor_scalar(b["ng"][:, q], b["mx"][:, q], -1.0, None, MUL).then_inc(s["soft_v"], 1)
        dve.tensor_tensor(b["sk"][:, q], sink, b["mx"][:, q], SUB).then_inc(s["soft_v"], 1)

    def out_low(m):
        dve.wait_ge(s["ao_hi"], m + 1)
        dve.tensor_tensor(b["aol"][:, m], b["ps"][:, 6 + m % 2], b["aoh"][:, m].bitcast(F32), SUB).then_inc(s["ao_lo"], 1)

    soft(0)
    soft(1)
    for m in range(PAIRS):
        q = m % 2
        dve.wait_ge(s["soft_a"], SOFT_A(m, "es"))
        dve.tensor_tensor(b["sk"][:, q], b["sk"][:, q], b["sum"][:, q], ADD).then_inc(s["normp_v"], 1)
        dve.wait_ge(s["normp_v"], NORMP_V(m, "den"))
        dve.reciprocal(b["sk"][:, q], b["sk"][:, q]).then_inc(s["normp_v"], 1)
        dve.wait_ge(s["normp_v"], NORMP_V(m, "rd"))
        dve.tensor_tensor(b["sm"][:, m % 3], b["sm"][:, m % 3], b["sk"][:, q, :, None].broadcast_to([P, 8, 256]), MUL) \
            .then_inc(s["normp_v"], 1)
        if m + 2 < PAIRS:
            soft(m + 2)
        if m:
            out_low(m - 1)
    out_low(PAIRS - 1)


MIX_P = Steps("ga0", "ga1", "gb0", "gb1", "ya0", "ya1", "yb0", "yb1")
MIX_A = Steps("ga0", "ga1", "gb0", "gb1")
MIX_V = Steps("a0", "a1", "b0", "b1", "m0", "m1")


def gated_pe(pe, s, b, ring, sources):
    for t in range(4):
        for i, (src, ready) in enumerate(sources):
            if t == 0 and ready:
                pe.wait_ge(*ready)
            for j in range(2):
                w = ring.take(pe)
                if t:
                    pe.wait_ge(*((s["gate_a"], 4 * (t - 1) + 2 * i + j + 1) if i < 2 else
                                 (s["gate_v"], MIX_V(t - 1, "ab"[i - 2] + str(j)))))
                split_matmuls(pe, b["ps"][:, 2 * i + j], columns_of(w, KD), src, KD).then_inc(s["gate_p"], 1)


def gated_act(act, s, b, high=None, first=0):
    for t in range(4):
        for i in range(4):
            if high:
                high.around(act, first + 8 * t + i)
            act.wait_ge(s["gate_p"], 8 * t + i + 1)
            if t:
                act.wait_ge(s["gate_v"], MIX_V(t - 1, f"m{i % 2}"))
            act.activation(b["sg"][:, i], b["ps"][:, i], ACT.Sigmoid).then_inc(s["gate_a"], 1)
        if high:
            for u in range(4, 8):
                high.around(act, first + 8 * t + u)


def gated_dve(dve, s, b, out):
    for t in range(4):
        for i in range(4):
            dve.wait_ge(s["gate_p"], 8 * t + 5 + i)
            dve.wait_ge(s["gate_a"], 4 * t + i + 1)
            dve.tensor_tensor(b["sg"][:, i], b["sg"][:, i], b["ps"][:, 4 + i], MUL).then_inc(s["gate_v"], 1)
        dve.wait_ge(s["gate_v"], MIX_V(t, "b1"))
        for j in range(2):
            dve.tensor_tensor(out[:, 2 * t + j], b["sg"][:, j], b["sg"][:, 2 + j], ADD).then_inc(s["gate_v"], 1)


def mixed_high_act(act, s, b):
    act.wait_ge(s["gate_p"], 8 * 3 + 4)
    for i in range(KD):
        act.wait_ge(s["gate_v"], MIX_V(i // 2, f"m{i % 2}"))
        act.activation(b["hh"][:, i], b["mixed"][:, i], ACT.Copy).then_inc(s["mx_hi"], 1)


def mixed_low_dve(dve, s, b):
    for i in range(KD):
        dve.wait_ge(s["mx_hi"], i + 1)
        dve.tensor_tensor(b["hl"][:, i], b["mixed"][:, i], b["hh"][:, i].bitcast(F32), SUB).then_inc(s["mx_lo"], 1)


def split_product(pe, ready, ps, w, b):
    for k in range(KD):
        if ready:
            pe.wait_ge(ready, k + 1)
        last = split_matmuls(pe, ps, columns_of(w, 1, at=k * P), tiles_of(b["hh"][:, k:k + 1], b["hl"][:, k:k + 1]), 1,
                             start=k == 0, stop=k == KD - 1)
    return last


def project_pe(pe, s, b, ring, done, copied, ready):
    for m in range(KD):
        w = ring.take(pe)
        if m >= 4:
            pe.wait_ge(copied, m - 3)
        split_product(pe, None if m else ready, b["ps"][:, m % 4], w, b).then_inc(done, 1)


def copy_act(act, b, mm, copied, dst, high, first, n=8, func=ACT.Copy):
    for m in range(n):
        high.around(act, first + m)
        act.wait_ge(mm, m + 1)
        act.activation(dst[:, m], b["ps"][:, m % 4], func).then_inc(copied, 1)


def residual_dve(dve, s, b, step, y, gain):
    for i in range(KD):
        if i >= 2:
            dve.wait_ge(step, 2 * (i - 1))
        dve.scalar_tensor_tensor(out=b["t2"][:, i % 2], in0=y[:, i], scalar=gain(i), in1=b["rstd"][:], op0=MUL, op1=MUL) \
            .then_inc(step, 1)
        dve.wait_ge(step, 2 * i + 1)
        dve.tensor_tensor(b["xT"][:, i], b["xT"][:, i], b["t2"][:, i % 2], ADD).then_inc(step, 1)


def scale_dve(dve, s, b, done, src, dst, gain, n=KD):
    for i in range(n):
        scaled(dve, b, src, gain)(i, dst[:, i]).then_inc(done, 1)


UP_A = Steps("za", "ca", "zb", "cb")
UP_V = Steps("a1", "a2", "b1", "b2")


def ffn_order(tiles, part_units):
    order, at = [], []
    u = 0
    def add(key, n=1):
        nonlocal u
        order.append(key)
        at.append(u)
        u += n
    parts = [list(range(i, min(i + PART, tiles))) for i in range(0, tiles, PART)]
    for i in range(tiles + 2):
        if i < tiles:
            for j in range(part_units):
                add(("up", i, j))
        for q, part in enumerate(parts):
            if i == part[-1] + 2 if part[-1] + 2 < tiles + 2 else False:
                for m in range(KD):
                    add(("down", q, m))
    return order, dict(zip(order, at)), u


def down_pe(pe, s, b, ring, part, m, tiles):
    n = min(PART, tiles - PART * part)
    w = ring.take(pe)
    g = PART * part
    if m == 0:
        pe.wait_ge(s["g_lo"], g + n)
    i = KD * part + m
    if i >= 3:
        pe.wait_ge(s["dn_v"], i - 2)
    right = [lambda k, x=x: x[:, (g + k) % GRING] for x in (b["gh"], b["gl"])]
    split_matmuls(pe, b["ps"][:, 4 + i % 3], columns_of(w, n), right, n).then_inc(s["dn_p"], 1)


FFN1 = ffn_order(FT, 2)


def ffn_pe(pe, s, b, ring):
    for key in FFN1[0]:
        if key[0] == "up":
            i, j = key[1:]
            w = ring.take(pe)
            if i >= 2:
                pe.wait_ge(s["up_a"], UP_A(i - 2, ("ca", "cb")[j]))
            split_product(pe, s["h2_lo"] if i == 0 and j == 0 else None, b["ps"][:, 2 * (i % 2) + j], w, b).then_inc(s["up_p"], 1)
        else:
            down_pe(pe, s, b, ring, key[1], key[2], FT)


def ffn_act(act, s, b, high, first):
    def gelu(i):
        act.wait_ge(s["up_v"], UP_V(i, "a2"))
        act.activation(b["acc"][:, 2 * (i % 2)], b["acc"][:, 2 * (i % 2)], ACT.Gelu_apprx_tanh).then_inc(s["up_ge"], 1)

    def g_high(i):
        act.wait_ge(s["up_g"], i + 1)
        if i >= GRING:
            act.wait_ge(s["dn_p"], KD * ((i - GRING) // PART + 1))
        act.activation(b["gh"][:, i % GRING], b["gt"][:, i % 2], ACT.Copy).then_inc(s["g_hi"], 1)

    for key in FFN1[0]:
        high.around(act, first + FFN1[1][key])
        if key[0] == "up":
            i, j = key[1:]
            act.wait_ge(s["up_p"], 2 * i + j + 1)
            slot = 2 * (i % 2) + j
            if i >= 2:
                act.wait_ge(s["up_v"], UP_V(i - 2, "ab"[j] + "2"))
                act.wait_ge(s["up_g"], i - 1)
            act.activation(b["cz"][:, slot, 2:TOK + 2], b["ps"][:, slot], ACT.Copy).then_inc(s["up_a"], 1)
            act.activation(b["acc"][:, slot], b["ps"][:, slot], ACT.Identity, scale=b["p"]("cw2", j * FT + i),
                           bias=b["p"]("cb", j * FT + i)).then_inc(s["up_a"], 1)
            if j == 1:
                if i:
                    gelu(i - 1)
                if i > 1:
                    g_high(i - 2)
                if i == FT - 1:
                    gelu(i)
                    g_high(i - 1)
                    g_high(i)


def down_dve(dve, s, b, part, m):
    i = KD * part + m
    dve.wait_ge(s["dn_p"], i + 1)
    ps = b["ps"][:, 4 + i % 3]
    if part == 0:
        dve.tensor_copy(b["yT"][:, m], ps).then_inc(s["dn_v"], 1)
    else:
        dve.tensor_tensor(b["yT"][:, m], b["yT"][:, m], ps, ADD).then_inc(s["dn_v"], 1)


def ffn_dve(dve, s, b):
    def product(i):
        dve.wait_ge(s["up_ge"], i + 1)
        dve.wait_ge(s["up_v"], UP_V(i, "b2"))
        if i >= 2:
            dve.wait_ge(s["g_lo"], i - 1)
        dve.tensor_tensor(b["gt"][:, i % 2], b["acc"][:, 2 * (i % 2)], b["acc"][:, 2 * (i % 2) + 1], MUL).then_inc(s["up_g"], 1)

    def g_low(i):
        dve.wait_ge(s["g_hi"], i + 1)
        dve.tensor_tensor(b["gl"][:, i % GRING], b["gt"][:, i % 2], b["gh"][:, i % GRING].bitcast(F32), SUB).then_inc(s["g_lo"], 1)

    for key in FFN1[0]:
        if key[0] == "down":
            down_dve(dve, s, b, key[1], key[2])
            continue
        i, j = key[1:]
        slot = 2 * (i % 2) + j
        dve.wait_ge(s["up_a"], UP_A(i, ("ca", "cb")[j]))
        dve.scalar_tensor_tensor(out=b["acc"][:, slot], in0=b["cz"][:, slot, 1:TOK + 1], scalar=b["p"]("cw1", j * FT + i),
                                 in1=b["acc"][:, slot], op0=MUL, op1=ADD).then_inc(s["up_v"], 1)
        dve.wait_ge(s["up_v"], UP_V(i, "ab"[j] + "1"))
        dve.scalar_tensor_tensor(out=b["acc"][:, slot], in0=b["cz"][:, slot, 0:TOK], scalar=b["p"]("cw0", j * FT + i),
                                 in1=b["acc"][:, slot], op0=MUL, op1=ADD).then_inc(s["up_v"], 1)
        if j == 1:
            if i:
                product(i - 1)
            if i > 1:
                g_low(i - 2)
            if i == FT - 1:
                product(i)
                g_low(i - 1)
                g_low(i)


def norms(*names):
    return [n + x for n in names for x in NORM_SEMS]


def freed_units1(s):
    out = [(s["lo_mm"], i + 1) for i in range(3)]
    for p in range(PAIRS):
        out += [(s["gemm_p"], GEMM(p, x)) for x in "rkva"]
    out += [(s["qkv_p"], i + 1) for i in range(10)] + [(s["qkv_p"], 14), (s["qkv_p"], 18)]
    out += [(s["gate_p"], i + 1) for i in range(32)]
    out += [(s["wo_p"], i + 1) for i in range(KD)]
    for key in FFN1[0]:
        out.append((s["up_p"], 2 * key[1] + key[2] + 1) if key[0] == "up" else (s["dn_p"], KD * key[1] + key[2] + 1))
    out += [(s["e_p"], 4), (s["e_p"], 8)] + [(s["pg_p"], i + 1) for i in range(KD)]
    return out


AT_ATT = 3 + 4 * PAIRS
AT_GATE = AT_ATT + 12
AT_WO = AT_GATE + 32
AT_FFN = AT_WO + KD
AT_E = AT_FFN + FFN1[2]
AT_PG = AT_E + 2
UNITS1 = AT_PG + KD
PARTS1 = -(-FT // PART)


def first_block(nc, b, stream, params, ple):
    names = [f"w_in{i}" for i in range(RAW)] + ["w_hi", "w_lo", "par_in", "ple_in", "zeroed", "x_out", "x_back"] + \
        norms("n1", "n2", "n3", "n4", "n5") + [n + x for n in ("h1", "h2") for x in SPLIT_SEMS] + \
        ["res1", "res2", "res3"] + RWKV_SEMS + ATT_SEMS + ["gate_p", "gate_a", "gate_v", "mx_hi", "mx_lo", "wo_p", "wo_z"] + \
        ["up_p", "up_a", "up_v", "up_ge", "up_g", "g_hi", "g_lo", "dn_p", "dn_v", "p_hi", "p_lo", "e_p", "e_z",
         "h3_hi", "h3_lo", "pg_p", "pg_z", "pg_v"]
    with ExitStack() as ctx:
        s, every = semaphores(ctx, nc, names)

        def sb(into, name, *shape, dt=F32):
            b[name] = into.enter_context(nc.sbuf_tensor(name, [P, *shape], dt))

        sb(ctx, "par", NPAR1)
        sb(ctx, "hh", KD, TOK, dt=F32R)
        sb(ctx, "hl", KD, TOK, dt=F32R)
        sb(ctx, "raw", RAW, UNIT)
        sb(ctx, "Whi", SLOTS, UNIT, dt=F32R)
        sb(ctx, "Wlo", SLOTS, UNIT, dt=F32R)
        b["p"] = lambda name, i: b["par"][:, PAR1[name] + i:PAR1[name] + i + 1]
        with ExitStack() as c:
            rwkv_buffers(c, nc, b)
        with ExitStack() as c:
            for name, *shape in (("t1", 2, TOK), ("t2", 2, TOK), ("sq", 2, TOK), ("rt", TOK), ("rstd", TOK)):
                sb(c, name, *shape)
            with ExitStack() as c2:
                for name in ("aoh", "aol"):
                    sb(c2, name, KD, TOK, dt=F32R)
                with ExitStack() as c3:
                    for name, *shape in (("qk", 10, TOK), ("vtok", BLK, 256), ("zr", 2, TOK), ("sm", 3, 8, 256),
                                         ("PT", BLK, 4, P), ("mx", 2, 8), ("ng", 2, 8), ("sk", 2, 8), ("sum", 2, 8)):
                        sb(c3, name, *shape)
                with ExitStack() as c3:
                    for name in ("yrh", "yrl"):
                        sb(c3, name, KD, TOK, dt=F32R)
                    sb(c3, "mixed", KD, TOK)
                    sb(c3, "sg", 4, TOK)
            with ExitStack() as c2:
                sb(c2, "yT", KD, TOK)
                with ExitStack() as c3:
                    for name in ("gh", "gl"):
                        sb(c3, name, GRING, TOK, dt=F32R)
                    for name, *shape in (("gt", 2, TOK), ("cz", 4, TOK + 2), ("acc", 4, TOK)):
                        sb(c3, name, *shape)
                with ExitStack() as c3:
                    sb(c3, "pT", 2, TOK)
                    sb(c3, "ph", 2, TOK, dt=F32R)
                    sb(c3, "pl", 2, TOK, dt=F32R)
                    sb(c3, "eT", KD, TOK)
        freed = freed_units1(s)
        assert len(freed) == UNITS1
        ffn_done = (s["dn_p"], KD * PARTS1)

        with nc.Fori(0, LAYERS) as layer:
            with nc.Block() as block:
                @block.sync
                def _(sp):
                    sp.dma_start(b["par"][:], params[bass.ds(layer, 1)].rearrange("l p n -> (l p) n")).then_inc(s["par_in"], 16)
                    stream_loads(sp, s, b, stream, layer, 0, 2)
                    sp.dma_start(b["park_x"], b["xT"][:]).then_inc(s["x_out"], 16)
                    stream_loads(sp, s, b, stream, layer, 2, AT_ATT + 2)
                    sp.wait_ge(s["x_out"], 16)
                    sp.wait_ge(s["tail_p"], TAIL_P(PAIRS - 1, "XA1"))
                    sp.dma_start(b["xT"][:], b["park_x"]).then_inc(s["x_back"], 16)
                    stream_loads(sp, s, b, stream, layer, AT_ATT + 2, AT_E + 2)
                    sp.wait_ge(*ffn_done)
                    sp.dma_start(b["pT"][:], ple[bass.ds(layer, 1)].rearrange("l p k n -> (l p) k n")).then_inc(s["ple_in"], 16)
                    stream_loads(sp, s, b, stream, layer, AT_E + 2, UNITS1)

                @block.gpsimd
                def _(pool):
                    pool.wait_ge(s["h1_lo"], KD)
                    for t in (b["zp"][:, :, 0:1], b["M"][:], b["N"][:], b["fe"][:]):
                        pool.memset(t, 0.0).then_inc(s["zeroed"], 1)
                    pool.wait_ge(s["x_out"], 16)
                    rwkv_pool(pool, s, b)
                    low_parts(pool, s, b, AT_ATT, AT_WO + 4)
                    pool.wait_ge(s["mx_lo"], KD)
                    pool.memset(b["cz"][:, :, 0:2], 0.0).then_inc(s["zeroed"], 1)
                    low_parts(pool, s, b, AT_WO + 4, AT_E + 2)
                    pool.wait_ge(s["p_hi"], 1)
                    pool.tensor_tensor(b["pl"][:], b["pT"][:], b["ph"][:].bitcast(F32), SUB).then_inc(s["p_lo"], 1)
                    low_parts(pool, s, b, AT_PG, AT_PG + 2)
                    for i in range(KD):
                        pool.wait_ge(s["h3_hi"], i + 1)
                        pool.tensor_tensor(b["hl"][:, i], b["xT"][:, i], b["hh"][:, i].bitcast(F32), SUB).then_inc(s["h3_lo"], 1)
                    low_parts(pool, s, b, AT_PG + 2, UNITS1)

                @block.tensor
                def _(pe):
                    ring = Ring(s, b)
                    h = tiles_of(b["hh"], b["hl"])
                    norm_pe(pe, s, b, "n1", KD)
                    rwkv_pe(pe, s, b, ring)
                    pe.wait_ge(s["post_a"], POST_A(PAIRS - 1, "sd"))
                    attention_pe(pe, s, b, ring)
                    gated_pe(pe, s, b, ring, ((h, None), (h, None), (tiles_of(b["aoh"], b["aol"]), (s["ao_lo"], PAIRS)),
                                              (tiles_of(b["yrh"], b["yrl"]), (s["y_back"], 32 * PAIRS))))
                    pe.wait_ge(s["gate_v"], MIX_V(3, "b1"))
                    project_pe(pe, s, b, ring, s["wo_p"], s["wo_z"], s["mx_lo"])
                    norm_pe(pe, s, b, "n2", KD)
                    norm_pe(pe, s, b, "n3", KD)
                    ffn_pe(pe, s, b, ring)
                    norm_pe(pe, s, b, "n4", KD)
                    for m in range(KD):
                        if m % 4 == 0:
                            w = ring.take(pe)
                        if m == 0:
                            pe.wait_ge(s["p_lo"], 1)
                        if m >= 4:
                            pe.wait_ge(s["e_z"], m - 3)
                        split_matmuls(pe, b["ps"][:, m % 4], columns_of(w, 2, width=512, j=m % 4 * P), tiles_of(b["ph"], b["pl"]), 2) \
                            .then_inc(s["e_p"], 1)
                    pe.wait_ge(s["e_z"], KD)
                    project_pe(pe, s, b, ring, s["pg_p"], s["pg_z"], s["h3_lo"])
                    norm_pe(pe, s, b, "n5", KD)

                @block.scalar
                def _(act):
                    high = HighParts(s, b, freed)
                    high.upto(act, 2)
                    norm_act(act, s, b, "n1", lambda i: b["xT"][:, i], KD, D, lambda i: (s["par_in"], 16))
                    split_act(act, s, "h1", b, b["hh"], KD)
                    act.wait_ge(s["zeroed"], 4)
                    rwkv_act(act, s, b, high)
                    attention_act(act, s, b, high)
                    gated_act(act, s, b, high, AT_GATE)
                    mixed_high_act(act, s, b)
                    copy_act(act, b, s["wo_p"], s["wo_z"], b["yT"], high, AT_WO)
                    norm_act(act, s, b, "n2", lambda i: b["yT"][:, i], KD, D, lambda i: (s["wo_z"], i + 1))
                    norm_act(act, s, b, "n3", lambda i: b["xT"][:, i], KD, D, lambda i: (s["res1"], 2 * i + 2))
                    split_act(act, s, "h2", b, b["hh"], KD)
                    act.wait_ge(s["zeroed"], 5)
                    ffn_act(act, s, b, high, AT_FFN)
                    norm_act(act, s, b, "n4", lambda i: b["yT"][:, i], KD, D, lambda i: (s["dn_v"], KD * (PARTS1 - 1) + i + 1))
                    act.wait_ge(s["ple_in"], 16)
                    act.activation(b["ph"][:], b["pT"][:], ACT.Copy).then_inc(s["p_hi"], 1)
                    for m in range(KD):
                        high.around(act, AT_E + m // 4)
                        act.wait_ge(s["e_p"], m + 1)
                        act.activation(b["eT"][:, m], b["ps"][:, m % 4], ACT.Copy).then_inc(s["e_z"], 1)
                    for i in range(KD):
                        act.wait_ge(s["res2"], 2 * i + 2)
                        act.activation(b["hh"][:, i], b["xT"][:, i], ACT.Copy).then_inc(s["h3_hi"], 1)
                    for m in range(KD):
                        high.around(act, AT_PG + m)
                        act.wait_ge(s["pg_p"], m + 1)
                        if m >= 2:
                            act.wait_ge(s["pg_v"], m - 1)
                        act.activation(b["t1"][:, m % 2], b["ps"][:, m % 4], ACT.Sigmoid).then_inc(s["pg_z"], 1)
                    norm_act(act, s, b, "n5", lambda i: b["yT"][:, i], KD, D, lambda i: (s["pg_v"], i + 1))

                @block.vector
                def _(dve):
                    norm_dve(dve, s, "n1", b)
                    split_dve(dve, s, "h1", b, scaled(dve, b, b["xT"], lambda i: b["p"]("mix_pre", i)), b["hh"], b["hl"], KD)
                    dve.wait_ge(s["zeroed"], 4)
                    rwkv_dve(dve, s, b)
                    attention_dve(dve, s, b)
                    gated_dve(dve, s, b, b["mixed"])
                    mixed_low_dve(dve, s, b)
                    norm_dve(dve, s, "n2", b)
                    dve.wait_ge(s["x_back"], 16)
                    residual_dve(dve, s, b, s["res1"], b["yT"], lambda i: b["p"]("mix_post", i))
                    norm_dve(dve, s, "n3", b)
                    split_dve(dve, s, "h2", b, scaled(dve, b, b["xT"], lambda i: b["p"]("ffn_pre", i)), b["hh"], b["hl"], KD)
                    ffn_dve(dve, s, b)
                    norm_dve(dve, s, "n4", b)
                    residual_dve(dve, s, b, s["res2"], b["yT"], lambda i: b["p"]("ffn_post", i))
                    for m in range(KD):
                        dve.wait_ge(s["pg_z"], m + 1)
                        dve.wait_ge(s["e_z"], m + 1)
                        dve.tensor_tensor(b["yT"][:, m], b["t1"][:, m % 2], b["eT"][:, m], MUL).then_inc(s["pg_v"], 1)
                    norm_dve(dve, s, "n5", b)
                    residual_dve(dve, s, b, s["res3"], b["yT"], lambda i: b["p"]("ple", i))
            clear_all(nc, every)



def matmuls(pe, ps, w, rhs, n, start=True, stop=True):
    last = None
    for k in range(n):
        last = pe.matmul(ps, w(k), rhs(k), start=start and k == 0, stop=stop and k == n - 1)
    return last


class Ring2:

    def __init__(self, s, b, first=0):
        self.s, self.b, self.u = s, b, first

    def take(self, pe):
        slot = self.u % SLOTS2
        pe.wait_ge(self.s[f"w2_in{slot}"], 16 * (self.u // SLOTS2 + 1))
        self.u += 1
        return self.b["W"][:, slot]


def stream_loads2(sp, s, b, dram, layer, freed):
    for u in range(len(freed)):
        if u >= SLOTS2:
            sp.wait_ge(*freed[u - SLOTS2])
        sp.dma_start(b["W"][:, u % SLOTS2], dram[bass.ds(layer, 1), u].rearrange("l p n -> (l p) n")) \
            .then_inc(s[f"w2_in{u % SLOTS2}"], 16)


def gated2_pe(pe, s, b, ring, sources, in_unit):
    for t in range(4):
        for i, (src, n) in enumerate(sources):
            if in_unit(i):
                unit, at = ring.take(pe), 0
            w = unit[:, at:at + 256 * n].rearrange("p (k n) -> p k n", k=n)
            at += 256 * n
            for j in range(2):
                if t:
                    pe.wait_ge(*((s["gate_a"], 4 * (t - 1) + 2 * i + j + 1) if i < 2 else
                                 (s["gate_v"], MIX_V(t - 1, "ab"[i - 2] + str(j)))))
                matmuls(pe, b["ps"][:, 2 * i + j], lambda k: w[:, k, j * P:(j + 1) * P], lambda k: src[:, k], n) \
                    .then_inc(s["gate_p"], 1)



Q_V = Steps("t1", "t2", "q")
SOFT2_V = Steps(*[f"a{n}" for n in range(4)], *[f"x{n}" for n in range(4)], "ng")
NORM2_V = Steps("rd", "p0", "p1", "p2", "p3", "o")
HEAD_SEMS = ["m_p", "md_v", "silu_a", "bada_v", "g1s", "h1", "h1x", "z_p", "z_z", "kr_p", "kr_a", "kr_v", "cqn", "ckvn", "uq_p", "uq_z",
             "perm_p", "rope_v", "uk_p", "uk_z", "uv_p", "uv_z", "kr_g", "score_p", "soft_v", "soft_a", "tr_p", "pt_a", "pv_p",
             "pn_v", "pool_s", "pool_m", "pool_d", "pm_p", "pm_z", "gate_p", "gate_a", "gate_v", "wo_p", "res1", "g2s",
             "f1_p", "f1_a", "f1_v", "g_hi", "g_lo", "dn_p", "dn_v", "mx_hi", "mx_lo", "w_in0", "w_in1", "w_hi", "w_lo",
             *["h2" + x for x in SPLIT_SEMS]]
KB2 = [n + 1 for n in range(BLK)]
KOFF = [0, 1, 3, 6]
SCALE2 = float(1.0 / np.sqrt(QK))


def mod_unit(j):
    if j < 8:
        return j
    if j < 18:
        return 8 + 3 * ((j - 8) // 2) + 1 + (j - 8) % 2
    return 23 + 4 * ((j - 18) // 3) + 1 + (j - 18) % 3


def mods_dve(dve, s, b, j):
    u = mod_unit(j)
    slot, acc = u % SLOTS2, b["macc"][:, j % 2]
    w = b["W"][:, slot].rearrange("p (k n) -> p k n", k=KD)
    dve.wait_ge(s[f"w2_in{slot}"], 16 * (u // SLOTS2 + 1))
    if j >= 2:
        dve.wait_ge(s["m_p"], 2 * (j - 1))
    for k in range(KD):
        if k == 0:
            dve.tensor_scalar(acc, w[:, k], b["cact"][:, k:k + 1], None, MUL).then_inc(s["md_v"], 1)
        else:
            dve.wait_ge(s["md_v"], KD * j + k)
            dve.scalar_tensor_tensor(out=acc, in0=w[:, k], scalar=b["cact"][:, k:k + 1], in1=acc, op0=MUL, op1=ADD) \
                .then_inc(s["md_v"], 1)


def mods_pe(pe, s, b, ring, first, n):
    for m in range(first, first + n):
        if m % 2 == 0:
            ring.u += 1
            pe.wait_ge(s["md_v"], KD * (m // 2 + 1))
        pe.matmul(b["ps"][:, 6, m:m + 1], b["macc"][:, m // 2 % 2, m % 2 * P:m % 2 * P + P], b["c"]("ones")[:, 0:1],
                  start=True, stop=True).then_inc(s["m_p"], 1)


def second_pe(pe, s, b, ring):
    norm_pe(pe, s, b, "n1", KD)
    mods_pe(pe, s, b, ring, 0, 16)
    for i in range(10):
        if i % 2 == 0:
            w = ring.take(pe).rearrange("p (k n) -> p k n", k=KD)
        if i >= 4:
            pe.wait_ge(s["z_z"], i - 3)
        wide = slice(64, 96) if i == 7 else slice(0, P)
        for k in range(KD):
            if i == 0:
                pe.wait_ge(s["h1x"], k + 1)
            last = pe.matmul(b["ps"][wide, i % 4], w[:, k, (i % 2) * P:(i % 2) * P + (32 if i == 7 else P)], b["hT"][:, k],
                             start=k == 0, stop=k == KD - 1)
        last.then_inc(s["z_p"], 1)
        mods_pe(pe, s, b, ring, 16 + 2 * i, 2)
    pe.wait_ge(s["z_z"], 10)
    pe.matmul(b["ps"][0:96, 4], b["c"]("perm2")[64:96], b["kr"][64:96], start=True, stop=True).then_inc(s["kr_p"], 1)
    norm_pe(pe, s, b, "nq", QT)
    norm_pe(pe, s, b, "nk", KVT)
    pe.wait_ge(s["cqn"], QT)
    for h in range(H2 + 1):
        if h < H2:
            if h % 4 == 0:
                w = ring.take(pe)[:, 0:QT * 4 * QK].rearrange("p (k n) -> p k n", k=QT)
            if h >= 4:
                pe.wait_ge(s["uq_z"], h - 3)
            matmuls(pe, b["ps"][0:QK, h % 4], lambda k: w[:, k, (h % 4) * QK:(h % 4 + 1) * QK], lambda k: b["cq"][:, k], QT) \
                .then_inc(s["uq_p"], 1)
            if h % 4:
                mods_pe(pe, s, b, ring, 36 + 2 * (h - 1 - h // 4), 2)
        if h:
            pe.wait_ge(s["uq_z"], h)
            if h >= 3:
                pe.wait_ge(s["rope_v"], Q_V(h - 3, "t2"))
            elif h == 1:
                pe.wait_ge(s["kr_v"], 2)
            pe.matmul(b["ps"][0:QK, 4 + (h - 1) % 2], b["c"]("perm2")[0:QK], b["zq"][0:QK, (h - 1) % 2], start=True, stop=True) \
                .then_inc(s["perm_p"], 1)
    unit = ring.take(pe)
    w = unit[:, 0:1024].rearrange("p (k n) -> p k n", k=KVT)
    pe.wait_ge(s["ckvn"], KVT)
    pe.wait_ge(s["uq_z"], H2)
    for h in range(H2):
        if h >= 4:
            pe.wait_ge(s["uk_z"], h - 3)
        matmuls(pe, b["ps"][0:NOPE, h % 4], lambda k: w[:, k, h * NOPE:(h + 1) * NOPE], lambda k: b["ckv"][:, k], KVT) \
            .then_inc(s["uk_p"], 1)
    wv = unit[:, 1024:2048].rearrange("p (k n) -> p k n", k=KVT)
    for t in range(BLK):
        pe.wait_ge(s["uk_z"], t + 5)
        matmuls(pe, b["ps"][:, t], lambda k: b["ckv"][:, k, t * P:(t + 1) * P], lambda k: wv[:, k], KVT).then_inc(s["uv_p"], 1)
    pe.wait_ge(s["uv_z"], BLK)
    pe.wait_ge(s["rope_v"], Q_V(H2 - 1, "q"))
    pe.wait_ge(s["kr_g"], H2)

    def scores(h):
        for n in range(BLK):
            if h:
                pe.wait_ge(s["soft_v"], SOFT2_V(h - 1, f"a{n}"))
            pe.matmul(b["ps"][:, n, 0:(n + 1) * P], b["qh"][0:QK, h, n * P:(n + 1) * P], b["kh2"][0:QK, h, 0:(n + 1) * P],
                      start=True, stop=True).then_inc(s["score_p"], 1)

    scores(0)
    scores(1)
    for h in range(H2):
        if h + 2 < H2:
            scores(h + 2)
        for n in range(BLK):
            pe.wait_ge(s["pn_v"], NORM2_V(h, f"p{n}"))
            if n >= 2 or h:
                pe.wait_ge(s["pt_a"], 4 * h + n - 1)
            for j in range(n + 1):
                last = pe.transpose(b["ps"][:, 4 + n % 2, j * P:(j + 1) * P], b["sm2"][:, h % 3, (KOFF[n] + j) * P:(KOFF[n] + j + 1) * P],
                                    b["c"]("ident"))
            last.then_inc(s["tr_p"], 1)
        if h % 2 == 0 and h >= 4:
            pe.wait_ge(s["pn_v"], NORM2_V(h - 3, "o"))
        for n in range(BLK):
            pe.wait_ge(s["pt_a"], 4 * h + n + 1)
            for j in range(n + 1):
                last = pe.matmul(b["ps"][half(h % 2), 6 + h // 2 % 2, n * P:(n + 1) * P], b["vtok2"][:, j, h * VD:(h + 1) * VD],
                                 b["PT2"][:, KOFF[n] + j], start=j == 0, stop=j == n)
        last.then_inc(s["pv_p"], 1)
    w = ring.take(pe)
    for g in range(4):
        pe.wait_ge(s["pool_d"], g + 1)
        pe.matmul(b["ps"][:, g], w[:, g * P:(g + 1) * P], b["pool"][:, g], start=True, stop=True).then_inc(s["pm_p"], 1)
    pe.wait_ge(s["pm_z"], 4)
    pe.wait_ge(s["pn_v"], NORM2_V(H2 - 1, "o"))
    gated2_pe(pe, s, b, ring, ((b["hT"], KD), (b["hT"], KD), (b["yp"], 4), (b["ao2"], 4)), lambda i: i != 3)
    pe.wait_ge(s["gate_v"], MIX_V(3, "b1"))
    ring = Ring(s, b)
    project_pe(pe, s, b, ring, s["wo_p"], s["res1"], s["mx_lo"])
    norm_pe(pe, s, b, "n2", KD)
    for key in FFN2[0]:
        if key[0] == "up":
            i = key[1]
            w = ring.take(pe)
            if i >= 4:
                pe.wait_ge(s["f1_a"], i - 3)
            split_product(pe, s["h2_lo"] if i == 0 else None, b["ps"][:, i % 4], w, b).then_inc(s["f1_p"], 1)
        else:
            down_pe(pe, s, b, ring, key[1], key[2], FT2)


def second_act(act, s, b):
    act.wait_ge(s["c_in"], 16)
    act.activation(b["cact"][:], b["cin"][:], ACT.Silu).then_inc(s["silu_a"], 1)
    norm_act(act, s, b, "n1", lambda i: b["xT"][:, i], KD, D, lambda i: (s["par_in"], 16))
    for i in range(KD):
        act.wait_ge(s["h1"], i + 1)
        act.activation(b["hT"][:, i], b["hT"][:, i], ACT.Identity, bias=b["mod"][:, i:i + 1]).then_inc(s["h1x"], 1)
    act.wait_ge(s["zeroed"], 1)
    for i in range(10):
        act.wait_ge(s["z_p"], i + 1)
        if i < 4:
            act.activation(b["u"][:, i, 16:16 + TOK], b["ps"][:, i % 4], ACT.Copy).then_inc(s["z_z"], 1)
        elif i == 7:
            act.activation(b["kr"][64:96], b["ps"][64:96, i % 4], ACT.Copy).then_inc(s["z_z"], 1)
        else:
            dst = b["cq"][:, i - 4] if i < 7 else b["ckv"][:, i - 8]
            act.activation(dst, b["ps"][:, i % 4], ACT.Copy).then_inc(s["z_z"], 1)
    norm_act(act, s, b, "nq", lambda i: b["cq"][:, i], QT, QT * P, lambda i: (s["z_z"], 10))
    norm_act(act, s, b, "nk", lambda i: b["ckv"][:, i], KVT, KVT * P, lambda i: (s["nq_rs"], 1))
    for h in range(H2):
        act.wait_ge(s["uq_p"], h + 1)
        if h >= 2:
            act.wait_ge(s["perm_p"], h - 1)
            act.wait_ge(s["rope_v"], Q_V(h - 2, "t1"))
        act.activation(b["zq"][0:QK, h % 2], b["ps"][0:QK, h % 4], ACT.Copy).then_inc(s["uq_z"], 1)
    for h in range(H2):
        act.wait_ge(s["uk_p"], h + 1)
        act.activation(b["kh2"][0:NOPE, h], b["ps"][0:NOPE, h % 4], ACT.Copy).then_inc(s["uk_z"], 1)
    for t in range(BLK):
        act.wait_ge(s["uv_p"], t + 1)
        act.activation(b["vtok2"][:, t], b["ps"][:, t], ACT.Copy).then_inc(s["uv_z"], 1)

    def exps(h):
        act.wait_ge(s["soft_v"], SOFT2_V(h, "ng"))
        if h >= 2:
            act.wait_ge(s["pn_v"], NORM2_V(h - 2, "rd"))
        for n in range(BLK):
            cols = slice(KOFF[n] * P, (KOFF[n] + n + 1) * P)
            act.activation(b["sm2"][:, h % 3, cols], b["sm2"][:, h % 3, cols], ACT.Exp, scale=SCALE2, bias=b["ng2"][:, h % 2, n:n + 1],
                           accum_out=b["sum2"][:, h % 2, n:n + 1]).then_inc(s["soft_a"], 1)

    exps(0)
    for h in range(H2):
        if h + 1 < H2:
            exps(h + 1)
        for n in range(BLK):
            act.wait_ge(s["tr_p"], 4 * h + n + 1)
            if h:
                act.wait_ge(s["pv_p"], h)
            act.activation(b["PT2"][:, KOFF[n]:KOFF[n] + n + 1].rearrange("k x q -> k (x q)"), b["ps"][:, 4 + n % 2, 0:(n + 1) * P],
                           ACT.Copy).then_inc(s["pt_a"], 1)
    for g in range(4):
        act.wait_ge(s["pm_p"], g + 1)
        act.activation(b["yp"][:, g], b["ps"][:, g], ACT.Copy, scale=b["p2"]("ps", g)).then_inc(s["pm_z"], 1)
    gated_act(act, s, b)
    high = HighParts(s, b, freed_units3(s))
    high.upto(act, SLOTS)
    mixed_high_act(act, s, b)
    for m in range(1, KD):
        high.around(act, m)
        act.wait_ge(s["wo_p"], m)
    norm_act(act, s, b, "n2", lambda i: b["xT"][:, i], KD, D, lambda i: (s["res1"], i + 1))
    split_act(act, s, "h2", b, b["hh"], KD, lambda i: b["mod"][:, 24 + i:25 + i])

    def g_high(i):
        act.wait_ge(s["f1_v"], i + 1)
        if i >= GRING:
            act.wait_ge(s["dn_p"], KD * ((i - GRING) // PART + 1))
        act.activation(b["gh"][:, i % GRING], b["gt"][:, i % 4], ACT.Copy).then_inc(s["g_hi"], 1)

    for key in FFN2[0]:
        high.around(act, KD + FFN2[1][key])
        if key[0] == "up":
            i = key[1]
            act.wait_ge(s["f1_p"], i + 1)
            if i >= 4:
                act.wait_ge(s["g_lo"], i - 3)
            act.activation(b["gt"][:, i % 4], b["ps"][:, i % 4], ACT.Relu).then_inc(s["f1_a"], 1)
            if i:
                g_high(i - 1)
            if i == FT2 - 1:
                g_high(i)


def second_dve(dve, s, b):
    dve.wait_ge(s["par_in"], 16)
    dve.wait_ge(s["silu_a"], 1)
    for j in range(8):
        mods_dve(dve, s, b, j)
    dve.wait_ge(s["m_p"], 16)
    dve.tensor_tensor(b["mod"][:, 0:16], b["ps"][:, 6, 0:16], b["p2s"]("bada", 0, 16), ADD).then_inc(s["bada_v"], 1)
    dve.wait_ge(s["bada_v"], 1)
    dve.scalar_tensor_tensor(out=b["gs"][:], in0=b["mod"][:, 8:16], scalar=1.0, in1=b["p2s"]("ln1", 0, 8), op0=ADD, op1=MUL) \
        .then_inc(s["g1s"], 1)
    dve.wait_ge(s["g1s"], 1)
    norm_dve(dve, s, "n1", b)
    scale_dve(dve, s, b, s["h1"], b["xT"], b["hT"], lambda i: b["gs"][:, i:i + 1])
    for j in range(8, 18):
        mods_dve(dve, s, b, j)
    r = slice(64, 96)
    dve.wait_ge(s["z_z"], 10)
    dve.tensor_tensor(b["krt"][r, 0], b["kr"][r], b["cos"][r], MUL).then_inc(s["kr_v"], 1)
    dve.wait_ge(s["kr_p"], 1)
    dve.tensor_tensor(b["krt"][r, 1], b["ps"][r, 4], b["sin"][r], MUL).then_inc(s["kr_v"], 1)
    dve.wait_ge(s["kr_v"], 2)
    dve.tensor_tensor(b["kr"][r], b["krt"][r, 0], b["krt"][r, 1], ADD).then_inc(s["kr_v"], 1)
    norm_dve(dve, s, "nq", b)
    scale_dve(dve, s, b, s["cqn"], b["cq"], b["cq"], lambda i: b["p2"]("qn", i), QT)
    dve.wait_ge(s["cqn"], QT)
    norm_dve(dve, s, "nk", b)
    scale_dve(dve, s, b, s["ckvn"], b["ckv"], b["ckv"], lambda i: b["p2"]("kvn", i), KVT)
    for h in range(H2):
        if (h + 1) % 4:
            mods_dve(dve, s, b, 18 + h - h // 4)
        dve.wait_ge(s["uq_z"], h + 1)
        if h >= 2:
            dve.wait_ge(s["rope_v"], Q_V(h - 2, "q"))
        dve.tensor_tensor(b["rot1"][0:QK, h % 2], b["zq"][0:QK, h % 2], b["cos"][0:QK], MUL).then_inc(s["rope_v"], 1)
        dve.wait_ge(s["perm_p"], h + 1)
        dve.tensor_tensor(b["rot2"][0:QK, h % 2], b["ps"][0:QK, 4 + h % 2], b["sin"][0:QK], MUL).then_inc(s["rope_v"], 1)
        dve.wait_ge(s["rope_v"], Q_V(h, "t2"))
        dve.tensor_tensor(b["qh"][0:QK, h], b["rot1"][0:QK, h % 2], b["rot2"][0:QK, h % 2], ADD).then_inc(s["rope_v"], 1)
    dve.wait_ge(s["m_p"], 48)
    dve.tensor_tensor(b["mod"][:, 16:48], b["ps"][:, 6, 16:48], b["p2s"]("bada", 16, 32), ADD).then_inc(s["bada_v"], 1)
    dve.wait_ge(s["bada_v"], 2)

    def soft(h):
        q = h % 2
        if h >= 3:
            dve.wait_ge(s["tr_p"], 4 * (h - 2))
        for n in range(BLK):
            cols = slice(KOFF[n] * P, (KOFF[n] + n + 1) * P)
            dve.wait_ge(s["score_p"], 4 * h + n + 1)
            dve.tensor_tensor(b["sm2"][:, h % 3, cols], b["ps"][:, n, 0:(n + 1) * P], b["c"]("cmask")[:, (3 - n) * P:TOK], ADD) \
                .then_inc(s["soft_v"], 1)
        for n in range(BLK):
            cols = slice(KOFF[n] * P, (KOFF[n] + n + 1) * P)
            dve.wait_ge(s["soft_v"], SOFT2_V(h, f"a{n}"))
            dve.tensor_reduce(b["ng2"][:, q, n:n + 1], b["sm2"][:, h % 3, cols], AX.X, MAX).then_inc(s["soft_v"], 1)
        dve.wait_ge(s["soft_v"], SOFT2_V(h, "x3"))
        dve.tensor_scalar(b["ng2"][:, q], b["ng2"][:, q], -SCALE2, None, MUL).then_inc(s["soft_v"], 1)

    soft(0)
    soft(1)
    for h in range(H2):
        q = h % 2
        dve.wait_ge(s["soft_a"], 4 * h + 4)
        dve.reciprocal(b["sum2"][:, q], b["sum2"][:, q]).then_inc(s["pn_v"], 1)
        dve.wait_ge(s["pn_v"], NORM2_V(h, "rd"))
        for n in range(BLK):
            cols = slice(KOFF[n] * P, (KOFF[n] + n + 1) * P)
            dve.tensor_scalar(b["sm2"][:, h % 3, cols], b["sm2"][:, h % 3, cols], b["sum2"][:, q, n:n + 1], None, MUL).then_inc(s["pn_v"], 1)
        if h + 2 < H2:
            soft(h + 2)
        dve.wait_ge(s["pv_p"], h + 1)
        dve.tensor_copy(b["ao2"][half(q), h // 2], b["ps"][half(q), 6 + h // 2 % 2]).then_inc(s["pn_v"], 1)
    gated_dve(dve, s, b, b["mixed"])
    mixed_low_dve(dve, s, b)
    for m in range(KD):
        dve.wait_ge(s["wo_p"], m + 1)
        dve.scalar_tensor_tensor(out=b["xT"][:, m], in0=b["ps"][:, m % 4], scalar=b["mod"][:, 16 + m:17 + m], in1=b["xT"][:, m],
                                 op0=MUL, op1=ADD).then_inc(s["res1"], 1)
    dve.scalar_tensor_tensor(out=b["gs"][:], in0=b["mod"][:, 32:40], scalar=1.0, in1=b["p2s"]("ln2", 0, 8), op0=ADD, op1=MUL) \
        .then_inc(s["g2s"], 1)
    dve.wait_ge(s["g2s"], 1)
    norm_dve(dve, s, "n2", b)
    split_dve(dve, s, "h2", b, scaled(dve, b, b["xT"], lambda i: b["gs"][:, i:i + 1]), b["hh"], b["hl"], KD,
              lambda i: b["mod"][:, 24 + i:25 + i])

    def g_low(i):
        dve.wait_ge(s["g_hi"], i + 1)
        dve.tensor_tensor(b["gl"][:, i % GRING], b["gt"][:, i % 4], b["gh"][:, i % GRING].bitcast(F32), SUB).then_inc(s["g_lo"], 1)

    for key in FFN2[0]:
        if key[0] == "up":
            i = key[1]
            dve.wait_ge(s["f1_a"], i + 1)
            dve.tensor_tensor(b["gt"][:, i % 4], b["gt"][:, i % 4], b["gt"][:, i % 4], MUL).then_inc(s["f1_v"], 1)
            if i:
                g_low(i - 1)
            if i == FT2 - 1:
                g_low(i)
        else:
            i, m = KD * key[1] + key[2], key[2]
            dve.wait_ge(s["dn_p"], i + 1)
            if i >= KD:
                dve.wait_ge(s["dn_v"], i - KD + 1)
            dve.scalar_tensor_tensor(out=b["xT"][:, m], in0=b["ps"][:, 4 + i % 3], scalar=b["mod"][:, 40 + m:41 + m], in1=b["xT"][:, m],
                                     op0=MUL, op1=ADD).then_inc(s["dn_v"], 1)


def second_pool(pool, s, b):
    pool.wait_ge(s["n1_rs"], 1)
    pool.memset(b["u"][:, :, 0:16], 0.0).then_inc(s["zeroed"], 1)
    pool.wait_ge(s["zeroed"], 1)
    sums = 0
    for g, w in enumerate(WINDOWS):
        pool.wait_ge(s["z_z"], g + 1)
        if g:
            pool.wait_ge(s["pool_d"], g)
        src = b["u"][:, g]
        for k in range(g + 1):
            lag, start, dst = 1 << k, 2 << k, b["win"][:, k % 2]
            pool.tensor_tensor(dst[:, start:16 + TOK], src[:, start:16 + TOK], src[:, start - lag:16 + TOK - lag], ADD) \
                .then_inc(s["pool_s"], 1)
            sums += 1
            pool.wait_ge(s["pool_s"], sums)
            src = dst
        pool.tensor_scalar(b["pool"][:, g, 16:TOK], src[:, 32:16 + TOK], 1.0 / w, None, MUL).then_inc(s["pool_m"], 1)
        pool.tensor_tensor(b["pool"][:, g, 0:16], src[:, 16:32], b["c"]("invcnt")[:, 16 * g:16 * g + 16], MUL).then_inc(s["pool_m"], 1)
        pool.wait_ge(s["pool_m"], 2 * g + 2)
        pool.tensor_tensor(b["pool"][:, g], b["pool"][:, g], b["u"][:, g, 16:16 + TOK], SUB).then_inc(s["pool_d"], 1)
    for h in range(H2):
        pool.wait_ge(s["kr_v"], 3)
        pool.wait_ge(*((s["kr_g"], h) if h else (s["pool_d"], 4)))
        pool.tensor_copy(b["kh2"][64:96, h], b["kr"][64:96]).then_inc(s["kr_g"], 1)


def freed_units2(s):
    summed = [(s["md_v"], KD * (j + 1)) for j in range(24)]
    out = summed[:8]
    for i in range(5):
        out += [(s["z_p"], 2 * i + 2)] + summed[8 + 2 * i:10 + 2 * i]
    for i in range(2):
        out += [(s["uq_p"], 4 * i + 4)] + summed[18 + 3 * i:21 + 3 * i]
    out += [(s["uv_p"], 4), (s["pm_p"], 4)]
    for t in range(4):
        out += [(s["gate_p"], 8 * t + 2), (s["gate_p"], 8 * t + 4), (s["gate_p"], 8 * t + 8)]
    return out


FFN2 = ffn_order(FT2, 1)
UNITS3 = KD + FFN2[2]


def freed_units3(s):
    out = [(s["wo_p"], i + 1) for i in range(KD)]
    return out + [(s["f1_p"], key[1] + 1) if key[0] == "up" else (s["dn_p"], KD * key[1] + key[2] + 1) for key in FFN2[0]]


def second_block(nc, b, stream, stream_b, params, cond):
    names = [f"w2_in{i}" for i in range(SLOTS2)] + ["par_in", "c_in", "zeroed"] + norms("n1", "n2", "nq", "nk") + HEAD_SEMS
    with ExitStack() as ctx:
        s, every = semaphores(ctx, nc, names)

        def sb(into, name, *shape, dt=F32):
            b[name] = into.enter_context(nc.sbuf_tensor(name + "_2", [P, *shape], dt))

        for name, *shape in (("W", SLOTS2, UNIT2), ("par2", NPAR2), ("cin", 8), ("cact", 8), ("macc", 2, 256), ("mod", MODS), ("gs", 8), ("sq", 2, TOK), ("rt", TOK),
                             ("rstd", TOK)):
            sb(ctx, name, *shape)
        b["p2"] = lambda name, i: b["par2"][:, PAR2[name] + i:PAR2[name] + i + 1]
        b["p2s"] = lambda name, i, n: b["par2"][:, PAR2[name] + i:PAR2[name] + i + n]
        with ExitStack() as c:
            sb(c, "gt", 4, TOK)
            sb(c, "t2", 2, TOK)
        sb(ctx, "hT", KD, TOK)
        with ExitStack() as c:
            for name, *shape in (("ao2", 4, TOK), ("pool", 4, TOK), ("yp", 4, TOK)):
                sb(c, name, *shape)
            with ExitStack() as c2:
                for name, *shape in (("u", 4, 16 + TOK), ("win", 2, 16 + TOK), ("cq", QT, TOK), ("ckv", KVT, TOK), ("kr", TOK),
                                     ("krt", 2, TOK), ("zq", 2, TOK), ("rot1", 2, TOK), ("rot2", 2, TOK), ("qh", H2, TOK),
                                     ("kh2", H2, TOK), ("vtok2", BLK, TOK), ("sm2", 3, 10 * P), ("PT2", 10, P), ("ng2", 2, 4),
                                     ("sum2", 2, 4)):
                    sb(c2, name, *shape)
            with ExitStack() as c2:
                sb(c2, "mixed", KD, TOK)
                sb(c2, "sg", 4, TOK)
                sb(c2, "raw", RAW, UNIT)
                sb(c2, "Whi", SLOTS, UNIT, dt=F32R)
                sb(c2, "Wlo", SLOTS, UNIT, dt=F32R)
                sb(c2, "hh", KD, TOK, dt=F32R)
                sb(c2, "hl", KD, TOK, dt=F32R)
        with ExitStack() as c:
            sb(c, "gh", GRING, TOK, dt=F32R)
            sb(c, "gl", GRING, TOK, dt=F32R)
        freed = freed_units2(s)
        with nc.Fori(0, LAYERS) as layer:
            with nc.Block() as block:
                @block.sync
                def _(sp):
                    sp.dma_start(b["par2"][:], params[bass.ds(layer, 1)].rearrange("l p n -> (l p) n")).then_inc(s["par_in"], 16)
                    sp.dma_start(b["cin"][:], cond).then_inc(s["c_in"], 16)
                    stream_loads2(sp, s, b, stream, layer, freed)
                    sp.wait_ge(s["gate_p"], 1)
                    stream_loads(sp, s, b, stream_b, layer, 0, UNITS3)

                @block.gpsimd
                def _(pool):
                    second_pool(pool, s, b)
                    low_parts(pool, s, b, 0, UNITS3)

                @block.tensor
                def _(pe):
                    second_pe(pe, s, b, Ring2(s, b))

                @block.scalar
                def _(act):
                    second_act(act, s, b)

                @block.vector
                def _(dve):
                    second_dve(dve, s, b)
            clear_all(nc, every)


def final_norm(nc, b, out):
    with ExitStack() as ctx:
        s, every = semaphores(ctx, nc, norms("nf") + ["y_done", "out_done"])
        for name, *shape in (("hT", KD, TOK), ("sq", 2, TOK), ("rt", TOK), ("rstd", TOK)):
            b[name] = ctx.enter_context(nc.sbuf_tensor(name + "_f", [P, *shape], F32))
        with nc.Block() as block:
            @block.scalar
            def _(act):
                norm_act(act, s, b, "nf", lambda i: b["xT"][:, i], KD, D)

            @block.tensor
            def _(pe):
                norm_pe(pe, s, b, "nf", KD)

            @block.vector
            def _(dve):
                norm_dve(dve, s, "nf", b)
                scale_dve(dve, s, b, s["y_done"], b["xT"], b["hT"], lambda i: b["fin"][:, i:i + 1])

            @block.sync
            def _(sp):
                for i in range(KD):
                    sp.wait_ge(s["y_done"], i + 1)
                    sp.dma_start(out[i * P:(i + 1) * P], b["hT"][:, i]).then_inc(s["out_done"], 16)
                sp.wait_ge(s["out_done"], 16 * KD)


def columns(v, rows=P):
    return np.ascontiguousarray(v.reshape(v.shape[0], -1, rows).transpose(0, 2, 1))


def unit_of(*parts, unit=UNIT):
    flat = [a.reshape(a.shape[0], P, -1) for a in parts]
    n = sum(a.shape[2] for a in flat)
    assert n <= unit
    return np.concatenate(flat + [np.zeros((flat[0].shape[0], P, unit - n), np.float32)], 2)


def ktiles(w, cols=slice(None)):
    w = w[:, :, cols]
    return w.reshape(w.shape[0], -1, P, w.shape[2]).transpose(0, 2, 1, 3)


def rows_up(w, n=P):
    return np.concatenate([w, np.zeros((w.shape[0], n - w.shape[1], w.shape[2]), w.dtype)], 1)


def layout1(a):
    L = LAYERS
    swap = np.arange(D).reshape(8, 2, 64)[:, ::-1].reshape(-1)
    order = [h for j in range(2) for g in range(4) for h in ((2 * j) * 4 + g, (2 * j + 1) * 4 + g)]
    qperm = np.concatenate([np.arange(h * 64, h * 64 + 64) for h in order])
    w = a["w_in"]
    q0, k0, v0, r0, g0 = 0, 1024, 1280, 1536, 1536 + 3360
    rw = r0
    lo0 = rw + 3072
    def tile(m, c, k=slice(None)):
        return unit_of(ktiles(m, slice(c, c + P))[:, :, k])

    last = np.zeros((L, P, KD, P), np.float32)
    last[..., :32] = ktiles(w, slice(lo0 + 256, lo0 + 288))
    units = [tile(w, lo0), tile(w, lo0 + P), unit_of(last)]
    wv = w[:, :, rw + 2048:rw + 3072][:, :, swap]
    g2 = a["rw_g2"][:, :, swap]
    none = np.zeros((L, 64, P), np.float32)
    for p in range(PAIRS):
        c = slice(p * P, p * P + P)
        units += [tile(w, rw + p * P), tile(w, rw + 1024 + p * P), tile(wv, p * P),
                  unit_of(np.concatenate([a["rw_w2"][:, :, c], none], 1), np.concatenate([none, a["rw_a2"][:, :, c]], 1),
                          g2[:, :P, c], rows_up(g2[:, P:, c]))]
    wq = w[:, :, q0:q0 + 1024][:, :, qperm]
    units += [tile(wq, P * i) for i in range(8)] + [tile(w, k0), tile(w, k0 + P), tile(w, v0), tile(w, v0 + P)]
    woa = a["w_o_att"][:, qperm]
    wor = a["w_o_rw"][:, swap]
    for t in range(4):
        for m, c in ((w, g0), (w, g0 + 1024), (woa, 0), (wor, 0)):
            units += [tile(m, c + 256 * t), tile(m, c + 256 * t + P)]
    units += [tile(a["w_out"], P * t) for t in range(KD)]
    for key in FFN1[0]:
        if key[0] == "up":
            units.append(tile(a["w_up"], key[2] * FFN + key[1] * P))
        else:
            units.append(tile(a["w_down"], key[2] * P, slice(PART * key[1], PART * key[1] + PART)))
    units += [unit_of(ktiles(a["w_ple"], slice(512 * i, 512 * i + 512))) for i in range(2)]
    units += [tile(a["w_ple_gate"], P * t) for t in range(KD)]
    assert len(units) == UNITS1
    stream = np.ascontiguousarray(np.stack(units, 1))

    mu = a["rw_mu"]
    mu_lo = np.concatenate([mu[:, 3072:3360], np.zeros((L, 96), np.float32)], 1)
    mu_all = np.concatenate([mu_lo, mu[:, :2048], mu[:, 2048:3072][:, swap]], 1)
    sink = a["att_sinks"][:, order].reshape(L, 8, 1, 2)
    sink = np.broadcast_to(sink, (L, 8, BLK, 2)).reshape(L, 1, 64)
    cw = a["conv_w"]
    cols = {"mix_pre": a["norm_mix_pre"], "mu": mu_all, "w0": a["rw_w0"], "a0": a["rw_a0"], "kk": a["rw_k_k"],
            "ka": a["rw_k_a"], "rk": a["rw_r_k"].reshape(L, D), "gnw": a["rw_gn_w"][:, swap], "gnb": a["rw_gn_b"][:, swap],
            "mix_post": a["norm_mix_post"], "ffn_pre": a["norm_ffn_pre"], "cw0": cw[:, 0], "cw1": cw[:, 1],
            "cw2": cw[:, 2], "cb": a["conv_b"], "ffn_post": a["norm_ffn_post"], "ple": a["norm_ple"]}
    params = np.concatenate([columns(cols[n]) for n in PAR1 if n != "sink"] + [np.broadcast_to(sink, (L, P, 64))], 2)
    ple = a["p"][:, 0].transpose(0, 2, 1).reshape(L, 2, P, TOK).transpose(0, 2, 1, 3)
    return {"stream1": stream, "params1": np.ascontiguousarray(params), "ple": np.ascontiguousarray(ple)}


def layout2(a):
    L = LAYERS

    def unit2(*parts):
        return unit_of(*parts, unit=UNIT2)

    two = lambda m, c: ktiles(m, slice(c, c + 256))
    ada, w = a["w_ada_2"], a["w_in_2"]
    more = [unit2(two(ada, 256 * i)) for i in range(8, 24)]
    kr = np.zeros((L, P, 8, 256), np.float32)
    kr[..., :128] = ktiles(w, slice(768, 896))
    kr[..., 128:160] = ktiles(w, slice(1152, 1184))
    units = [unit2(two(ada, 256 * i)) for i in range(8)]
    for i, unit in enumerate((unit2(two(w, 0)), unit2(two(w, 256)), unit2(two(w, 512)), unit2(kr), unit2(two(w, 896)))):
        units += [unit] + more[2 * i:2 * i + 2]
    uq = a["w_uq_2"].reshape(L, QT * P, H2 * QK)
    for i in range(2):
        units += [unit2(ktiles(uq, slice(384 * i, 384 * i + 384)))] + more[10 + 3 * i:13 + 3 * i]
    units.append(unit2(ktiles(a["w_uk_2"].reshape(L, 256, 512)), ktiles(a["w_uv_2"].reshape(L, 256, 512))))
    units.append(unit2(a["w_pool_2"].transpose(0, 2, 1, 3)))
    for t in range(4):
        units += [unit2(two(w, 1184 + 256 * t)), unit2(two(w, 2208 + 256 * t)),
                  unit2(two(a["p_pool_2"], 256 * t), two(a["p_attn_2"], 256 * t))]

    def tile(m, c, k=slice(None)):
        return unit_of(ktiles(m, slice(c, c + P))[:, :, k])

    split = [tile(a["w_out_2"], P * t) for t in range(KD)]
    for key in FFN2[0]:
        split.append(tile(a["w_ff1_2"], key[1] * P) if key[0] == "up" else
                     tile(a["w_ff2_2"], key[2] * P, slice(PART * key[1], PART * key[1] + PART)))
    assert len(split) == UNITS3
    cols = {"ln1": a["ln1_g_2"], "ln2": a["ln2_g_2"], "bada": a["b_ada_2"], "qn": a["q_norm_g_2"], "kvn": a["kv_norm_g_2"],
            "ps": a["pool_scale_2"]}
    return {"stream2": np.ascontiguousarray(np.stack(units, 1)), "stream3": np.ascontiguousarray(np.stack(split, 1)),
            "params2": np.ascontiguousarray(np.concatenate([columns(cols[n]) for n in PAR2], 2)),
            "cond": columns(a["c_2"])[0], "final": columns(a["final_g_2"][None])[0]}


def constants():
    f = np.float32
    i = np.arange(P)
    c = {}
    c["ident"] = np.eye(P)
    c["ones"] = np.ones((P, P))
    c["bd"] = (i[:, None] // 64 == i[None] // 64)
    c["bdswap"] = (i[:, None] // 64 != i[None] // 64)
    lv = []
    for l in range(LEVELS):
        n = 1 << l
        same = i[:, None] // (2 * n) == i[None] // (2 * n)
        lv.append(same & (i[:, None] % (2 * n) < n) & (i[None] % (2 * n) >= n))
    c["lvl"] = np.concatenate(lv, 1)
    c["tmask"] = np.concatenate([i[:, None] < i[None], i[:, None] <= i[None]], 1)
    j = np.arange(256)
    dist = i[:, None] + P - j[None]
    c["amask"] = np.where((dist >= 0) & (dist < P), 0.0, NEG)
    c["cmask"] = np.concatenate([np.zeros((P, 384)), np.where(i[:, None] >= i[None], 0.0, NEG)], 1)
    perm1 = np.zeros((P, P))
    for m in range(P):
        if m % 64 < 32:
            perm1[m + 32, m] = -1.0
        else:
            perm1[m - 32, m] = 1.0
    c["perm1"] = perm1
    perm2 = np.zeros((P, 96))
    for m in range(64, 96):
        if m < 80:
            perm2[m + 16, m] = -1.0
        else:
            perm2[m - 16, m] = 1.0
    c["perm2"] = perm2
    c["freq1"] = np.power(f(10000.0), -(np.arange(32, dtype=f)) / f(32))[i % 32][:, None]
    c["freq2"] = np.where(i < 64, f(0), np.power(f(10000.0), -(np.arange(0, 32, 2, dtype=f)) / f(32))[i % 16])[:, None]
    t = np.arange(16)
    c["invcnt"] = np.broadcast_to(np.concatenate([1.0 / np.minimum(t + 1, w) for w in WINDOWS])[None], (P, 64))
    c["eps6"] = np.full((P, 1), 1e-6)
    c["epsgn"] = np.full((P, 1), GN_EPS)
    return np.ascontiguousarray(np.concatenate([np.asarray(c[n], f) for n in CONST], 1))


def prologue(nc, b, x, const, final_gain):
    with ExitStack() as ctx:
        s, every = semaphores(ctx, nc, ["x_in", "const_in", "gain_in"])
        with nc.Block() as block:
            @block.sync
            def _(sp):
                sp.dma_start(b["const"][:], const).then_inc(s["const_in"], 16)
                sp.dma_start(b["xT"][:], x.rearrange("(k p) t -> p k t", p=P)).then_inc(s["x_in"], 16)
                sp.dma_start(b["fin"][:], final_gain).then_inc(s["gain_in"], 16)
                sp.wait_ge(s["x_in"], 16)
                sp.wait_ge(s["gain_in"], 16)
                sp.wait_ge(s["const_in"], 16)
        clear_all(nc, every)


def shared_buffers(ctx, nc):
    b = {}
    for name, *shape in (("const", NCONST), ("fin", KD), ("cos", TOK), ("sin", TOK)):
        b[name] = ctx.enter_context(nc.sbuf_tensor(name, [P, *shape], F32))
    with ExitStack() as c:
        for name, *shape in (("TM", 2, 2, TOK), ("X", 2, TOK), ("XT", 2, TOK)):
            b[name] = c.enter_context(nc.sbuf_tensor(name, [P, *shape], F32))
    b["xT"] = ctx.enter_context(nc.sbuf_tensor("xT", [P, KD, TOK], F32))
    b["park_x"] = nc.dram_tensor("park_x", [P, KD, TOK], F32, kind="Internal").ap()
    b["park_yh"] = nc.dram_tensor("park_yh", [PAIRS, P, TOK], F32, kind="Internal").ap()
    b["park_yl"] = nc.dram_tensor("park_yl", [PAIRS, P, TOK], F32, kind="Internal").ap()
    b["norm_bank"] = 7
    b["ps"] = ctx.enter_context(nc.psum_tensor("ps", [P, 8, TOK], F32))
    ends = list(CONST.values())[1:] + [NCONST]
    width = {n: e - a for (n, a), e in zip(CONST.items(), ends)}
    b["c"] = lambda name: b["const"][:, CONST[name]:CONST[name] + width[name]]
    return b


def build(nc, t, out):
    with ExitStack() as ctx:
        b = shared_buffers(ctx, nc)
        prologue(nc, b, t["x"], t["const"], t["final"])
        tables(nc, b, t["pos1"], "freq1", slice(0, P), b["cos"][:], b["sin"][:])
        first_block(nc, b, t["stream1"], t["params1"], t["ple"])
        tables(nc, b, t["pos2"], "freq2", slice(0, P), b["cos"][:], b["sin"][:])
        second_block(nc, b, t["stream2"], t["stream3"], t["params2"], t["cond"])
        final_norm(nc, b, out)


def kernel(**inputs):
    import concourse.bacc as bacc
    from concourse.bass_utils import run_bass_kernel_spmd

    a = {n: np.asarray(v) for n, v in inputs.items()}
    data = {"x": np.ascontiguousarray(a["x"][0].T), "const": constants(), "pos1": a["positions"], "pos2": a["positions_2"],
            **layout1(a), **layout2(a)}
    nc = bacc.Bacc("TRN2", target_bir_lowering=False, num_devices=1)
    arrays = {f"in_{n}": np.ascontiguousarray(v) for n, v in data.items()}
    t = {n: nc.dram_tensor(f"in_{n}", v.shape, mybir.dt.from_np(v.dtype), kind="ExternalInput").ap() for n, v in data.items()}
    out = nc.dram_tensor("out", [D, TOK], F32, kind="ExternalOutput").ap()
    build(nc, t, out)
    got = run_bass_kernel_spmd(nc, [arrays], core_ids=[0]).results[0]["out"]
    return np.ascontiguousarray(got.T)[None]
```
